# Optimizing a Trainium2 kernel written in Bass

```python
import jax, jax.numpy as jnp
from jax import lax
import numpy as np

D_MODEL = 1024
BATCH = 1
SEQ = 256
DEPTH = 1

RNN_WIDTH = 512
RNN_BLOCKS = 8
RNN_BLOCK = RNN_WIDTH // RNN_BLOCKS
RNN_CONV = 4
RG_C = 8.0
NSA_HEADS = 8
NSA_KV_HEADS = 2
HEAD_DIM = 64
NSA_GROUP = NSA_HEADS // NSA_KV_HEADS
NSA_WIDTH = NSA_HEADS * HEAD_DIM
KV_WIDTH = NSA_KV_HEADS * HEAD_DIM
N_NSA_BRANCHES = 3
CMP_LEN = 32
CMP_STRIDE = 16
CMP_HIDDEN = 128
SEL_LEN = 64
SEL_TOPK = 16
WINDOW = 512
Q_BLOCK = 128
SC_WIDTH = 512
SC_CONV = 3
N_MIXERS = 3
N_GROUPS = 4
EXPERTS_PER_GROUP = 8
N_EXPERTS = N_GROUPS * EXPERTS_PER_GROUP
EXPERT_HIDDEN = 256
TOPK_IN_GROUP = 2

IN_SPLITS = (RNN_WIDTH, RNN_WIDTH, NSA_WIDTH) + (KV_WIDTH,) * 6 + (NSA_HEADS * N_NSA_BRANCHES,) + (SC_WIDTH,) * 3 + (N_MIXERS * D_MODEL,)
IN_WIDTH = sum(IN_SPLITS)

RMS_EPS = 1e-6
NEG_INF = -1e30
FORCE_SCORE = 1e6

kernel_name = 'hybrid_rglru_nsa_shortconv_hmoe'

def _split_points():
    return [int(v) for v in np.cumsum(IN_SPLITS)[:-1]]

def rms_norm(x, gain):
    xf = x.astype(jnp.float32)
    y = xf * lax.rsqrt(jnp.mean(xf * xf, axis=-1, keepdims=True) + RMS_EPS)
    return (y * gain.astype(jnp.float32)).astype(x.dtype)

def causal_depthwise_conv(x, w):
    k, c = w.shape
    return lax.conv_general_dilated(
        x, w[:, None, :].astype(x.dtype), window_strides=(1,), padding=[(k - 1, 0)],
        dimension_numbers=('NWC', 'WIO', 'NWC'), feature_group_count=c)

def rg_lru(x, wa, ba, wx, bx, lam):
    b, s, _ = x.shape
    xb = x.reshape(b, s, RNN_BLOCKS, RNN_BLOCK)
    r = jax.nn.sigmoid(jnp.einsum('bsni,nij->bsnj', xb, wa) + ba).reshape(b, s, RNN_WIDTH)
    i = jax.nn.sigmoid(jnp.einsum('bsni,nij->bsnj', xb, wx) + bx).reshape(b, s, RNN_WIDTH)
    log_a = -RG_C * r.astype(jnp.float32) * jax.nn.softplus(-lam.astype(jnp.float32))
    a = jnp.exp(log_a)
    mult = jnp.sqrt(-jnp.expm1(2.0 * log_a))
    u = mult * (i * x).astype(jnp.float32)

    def combine(left, right):
        a1, b1 = left
        a2, b2 = right
        return a1 * a2, a2 * b1 + b2

    _, h = lax.associative_scan(combine, (a, u), axis=1)
    return h.astype(x.dtype)

def compress_blocks(k, pe, w1, b1, w2, b2):
    b, s = k.shape[:2]
    n_cmp = (s - CMP_LEN) // CMP_STRIDE + 1
    idx = jnp.arange(n_cmp)[:, None] * CMP_STRIDE + jnp.arange(CMP_LEN)[None, :]
    blocks = k[:, idx] + pe[None, None, :, None, :]
    blocks = blocks.transpose(0, 1, 3, 2, 4).reshape(b, n_cmp, NSA_KV_HEADS, CMP_LEN * HEAD_DIM)
    hid = jax.nn.gelu(blocks @ w1 + b1)
    return hid @ w2 + b2

def native_sparse_attention(q, k_cmp, v_cmp, k_sel, v_sel, k_win, v_win, gates):
    f32 = jnp.float32
    b, s = q.shape[:2]
    n_chunks = s // Q_BLOCK
    n_cmp = k_cmp.shape[1]
    n_sel = s // SEL_LEN
    top_k = min(SEL_TOPK, n_sel)
    scale = HEAD_DIM ** -0.5
    k_cmp = k_cmp.astype(f32)
    v_cmp = v_cmp.astype(f32)
    cmp_start = jnp.arange(n_cmp) * CMP_STRIDE
    cmp_end = cmp_start + CMP_LEN
    sel_start = jnp.arange(n_sel) * SEL_LEN
    overlap = jnp.clip(jnp.minimum(cmp_end[:, None], sel_start[None, :] + SEL_LEN)
                       - jnp.maximum(cmp_start[:, None], sel_start[None, :]), 0).astype(f32) / CMP_LEN
    ks_blk = k_sel.astype(f32).reshape(b, n_sel, SEL_LEN, NSA_KV_HEADS, HEAD_DIM).transpose(0, 3, 1, 2, 4)
    vs_blk = v_sel.astype(f32).reshape(b, n_sel, SEL_LEN, NSA_KV_HEADS, HEAD_DIM).transpose(0, 3, 1, 2, 4)
    pad = jnp.zeros((b, WINDOW, NSA_KV_HEADS, HEAD_DIM), f32)
    kw_pad = jnp.concatenate([pad, k_win.astype(f32)], axis=1)
    vw_pad = jnp.concatenate([pad, v_win.astype(f32)], axis=1)
    bi = jnp.arange(b)[:, None, None, None]
    gi = jnp.arange(NSA_KV_HEADS)[None, :, None, None]
    j = jnp.arange(n_sel)

    def query_block(c):
        t0 = c * Q_BLOCK
        t = t0 + jnp.arange(Q_BLOCK)
        qc = lax.dynamic_slice_in_dim(q, t0, Q_BLOCK, axis=1).astype(f32)
        s_c = jnp.einsum('btghd,bngd->bghtn', qc, k_cmp) * scale
        m_c = cmp_end[None, :] - 1 <= t[:, None]
        p_c = jax.nn.softmax(jnp.where(m_c, s_c, NEG_INF), axis=-1)
        p_c = p_c * jnp.any(m_c, axis=-1)[:, None].astype(f32)
        o_c = jnp.einsum('bghtn,bngd->btghd', p_c, v_cmp)
        imp = jnp.einsum('bghtn,nj->bgtj', p_c, overlap)
        cur = t // SEL_LEN
        causal_j = j[None, :] <= cur[:, None]
        forced = (j[None, :] == 0) | (j[None, :] == cur[:, None]) | (j[None, :] == cur[:, None] - 1)
        imp = jnp.where(forced, FORCE_SCORE, imp)
        imp = jnp.where(causal_j, imp, -1.0)
        top_val, top_idx = lax.top_k(imp, top_k)
        blk_ok = top_val >= 0.0
        kg = ks_blk[bi, gi, top_idx]
        vg = vs_blk[bi, gi, top_idx]
        pos = top_idx[..., None] * SEL_LEN + jnp.arange(SEL_LEN)
        m_s = blk_ok[..., None] & (pos <= t[None, None, :, None, None])
        s_s = jnp.einsum('btghd,bgtkld->bghtkl', qc, kg) * scale
        s_s = jnp.where(m_s[:, :, None], s_s, NEG_INF).reshape(b, NSA_KV_HEADS, NSA_GROUP, Q_BLOCK, top_k * SEL_LEN)
        p_s = jax.nn.softmax(s_s, axis=-1).reshape(b, NSA_KV_HEADS, NSA_GROUP, Q_BLOCK, top_k, SEL_LEN)
        o_s = jnp.einsum('bghtkl,bgtkld->btghd', p_s, vg)
        kwc = lax.dynamic_slice_in_dim(kw_pad, t0, Q_BLOCK + WINDOW, axis=1)
        vwc = lax.dynamic_slice_in_dim(vw_pad, t0, Q_BLOCK + WINDOW, axis=1)
        spos = t0 - WINDOW + jnp.arange(Q_BLOCK + WINDOW)
        diff = t[:, None] - spos[None, :]
        m_w = (diff >= 0) & (diff < WINDOW) & (spos[None, :] >= 0)
        s_w = jnp.einsum('btghd,bsgd->bghts', qc, kwc) * scale
        p_w = jax.nn.softmax(jnp.where(m_w, s_w, NEG_INF), axis=-1)
        o_w = jnp.einsum('bghts,bsgd->btghd', p_w, vwc)
        gc = lax.dynamic_slice_in_dim(gates, t0, Q_BLOCK, axis=1).astype(f32)
        o = gc[..., 0:1] * o_c + gc[..., 1:2] * o_s + gc[..., 2:3] * o_w
        return o.reshape(b, Q_BLOCK, NSA_WIDTH)

    out = lax.map(query_block, jnp.arange(n_chunks))
    return out.transpose(1, 0, 2, 3).reshape(b, s, NSA_WIDTH).astype(q.dtype)

def hierarchical_moe(x, wg, bg, we, be, w_gate, w_up, w_down):
    f32 = jnp.float32
    b, s, d = x.shape
    n = b * s
    xt = x.reshape(n, d)
    g_logits = (xt @ wg).astype(f32) + bg.astype(f32)
    g_prob = jax.nn.softmax(g_logits, axis=-1)
    grp = jnp.argmax(g_logits, axis=-1)
    tok = jnp.arange(n)
    p_grp = g_prob[tok, grp][:, None]
    e_logits = ((xt @ we).astype(f32) + be.astype(f32)).reshape(n, N_GROUPS, EXPERTS_PER_GROUP)
    e_prob = jax.nn.softmax(e_logits[tok, grp], axis=-1)
    top_p, top_i = lax.top_k(e_prob, TOPK_IN_GROUP)
    weights = p_grp * top_p / jnp.sum(top_p, axis=-1, keepdims=True)
    expert_id = grp[:, None] * EXPERTS_PER_GROUP + top_i
    combine = jnp.einsum('nke,nk->ne', jax.nn.one_hot(expert_id, N_EXPERTS, dtype=f32), weights)
    y = jnp.zeros((n, d), f32)
    for g in range(N_GROUPS):
        e0 = g * EXPERTS_PER_GROUP
        e1 = e0 + EXPERTS_PER_GROUP
        h = jax.nn.silu(jnp.einsum('nd,edf->nef', xt, w_gate[e0:e1])) * jnp.einsum('nd,edf->nef', xt, w_up[e0:e1])
        h = h * combine[:, e0:e1, None].astype(h.dtype)
        y = y + jnp.einsum('nef,efd->nd', h, w_down[e0:e1])
    return y.reshape(b, s, d).astype(x.dtype)

def setup_inputs(seed: int = 0) -> dict:
    key = jax.random.key(seed)
    ks = jax.random.split(key, 30)
    L = DEPTH

    def nrm(k, shape, scale):
        return jax.random.normal(k, shape, jnp.float32) * scale

    u = jax.random.uniform(ks[9], (L, RNN_WIDTH), jnp.float32, 0.9, 0.999)
    p = u ** (1.0 / RG_C)
    return {
        'x': nrm(ks[0], (BATCH, SEQ, D_MODEL), 1.0),
        'mix_norm': 1.0 + nrm(ks[1], (L, D_MODEL), 0.05),
        'w_in': nrm(ks[2], (L, D_MODEL, IN_WIDTH), D_MODEL ** -0.5),
        'rnn_conv_w': nrm(ks[3], (L, RNN_CONV, RNN_WIDTH), RNN_CONV ** -0.5),
        'rnn_conv_b': nrm(ks[4], (L, RNN_WIDTH), 0.01),
        'rg_wa': nrm(ks[5], (L, RNN_BLOCKS, RNN_BLOCK, RNN_BLOCK), RNN_BLOCK ** -0.5),
        'rg_ba': nrm(ks[6], (L, RNN_BLOCKS, RNN_BLOCK), 0.01),
        'rg_wx': nrm(ks[7], (L, RNN_BLOCKS, RNN_BLOCK, RNN_BLOCK), RNN_BLOCK ** -0.5),
        'rg_bx': nrm(ks[8], (L, RNN_BLOCKS, RNN_BLOCK), 0.01),
        'rg_lambda': jnp.log(p) - jnp.log1p(-p),
        'cmp_pe': nrm(ks[10], (L, 2, CMP_LEN, HEAD_DIM), 0.1),
        'cmp_w1': nrm(ks[11], (L, 2, CMP_LEN * HEAD_DIM, CMP_HIDDEN), (CMP_LEN * HEAD_DIM) ** -0.5),
        'cmp_b1': nrm(ks[12], (L, 2, CMP_HIDDEN), 0.01),
        'cmp_w2': nrm(ks[13], (L, 2, CMP_HIDDEN, HEAD_DIM), CMP_HIDDEN ** -0.5),
        'cmp_b2': nrm(ks[14], (L, 2, HEAD_DIM), 0.01),
        'q_norm': 1.0 + nrm(ks[15], (L, HEAD_DIM), 0.05),
        'k_norm': 1.0 + nrm(ks[16], (L, N_NSA_BRANCHES, HEAD_DIM), 0.05),
        'sc_conv_w': nrm(ks[17], (L, SC_CONV, SC_WIDTH), SC_CONV ** -0.5),
        'w_rnn_out': nrm(ks[18], (L, RNN_WIDTH, D_MODEL), RNN_WIDTH ** -0.5),
        'w_nsa_out': nrm(ks[19], (L, NSA_WIDTH, D_MODEL), NSA_WIDTH ** -0.5),
        'w_sc_out': nrm(ks[20], (L, SC_WIDTH, D_MODEL), SC_WIDTH ** -0.5),
        'w_out': nrm(ks[21], (L, D_MODEL, D_MODEL), D_MODEL ** -0.5),
        'ffn_norm': 1.0 + nrm(ks[22], (L, D_MODEL), 0.05),
        'router_group_w': nrm(ks[23], (L, D_MODEL, N_GROUPS), D_MODEL ** -0.5),
        'router_group_b': nrm(ks[24], (L, N_GROUPS), 0.01),
        'router_expert_w': nrm(ks[25], (L, D_MODEL, N_EXPERTS), D_MODEL ** -0.5),
        'router_expert_b': nrm(ks[26], (L, N_EXPERTS), 0.01),
        'exp_w_gate': nrm(ks[27], (L, N_EXPERTS, D_MODEL, EXPERT_HIDDEN), D_MODEL ** -0.5),
        'exp_w_up': nrm(ks[28], (L, N_EXPERTS, D_MODEL, EXPERT_HIDDEN), D_MODEL ** -0.5),
        'exp_w_down': nrm(ks[29], (L, N_EXPERTS, EXPERT_HIDDEN, D_MODEL), EXPERT_HIDDEN ** -0.5),
    }

def reference(x, mix_norm, w_in, rnn_conv_w, rnn_conv_b, rg_wa, rg_ba, rg_wx, rg_bx, rg_lambda,
              cmp_pe, cmp_w1, cmp_b1, cmp_w2, cmp_b2, q_norm, k_norm, sc_conv_w,
              w_rnn_out, w_nsa_out, w_sc_out, w_out, ffn_norm,
              router_group_w, router_group_b, router_expert_w, router_expert_b,
              exp_w_gate, exp_w_up, exp_w_down):
    b, s, _ = x.shape
    split_points = _split_points()
    for l in range(DEPTH):
        xn = rms_norm(x, mix_norm[l])
        (rnn_x, rnn_y, q, kc, vc, ksl, vsl, kwn, vwn, nsa_g,
         sc_b, sc_c, sc_h, merge_g) = jnp.split(xn @ w_in[l], split_points, axis=-1)

        u = causal_depthwise_conv(rnn_x, rnn_conv_w[l]) + rnn_conv_b[l]
        y_rnn = jax.nn.gelu(rnn_y) * rg_lru(u, rg_wa[l], rg_ba[l], rg_wx[l], rg_bx[l], rg_lambda[l])

        qh = rms_norm(q.reshape(b, s, NSA_HEADS, HEAD_DIM), q_norm[l])
        qh = qh.reshape(b, s, NSA_KV_HEADS, NSA_GROUP, HEAD_DIM)
        kv_shape = (b, s, NSA_KV_HEADS, HEAD_DIM)
        k_cmp = rms_norm(compress_blocks(kc.reshape(kv_shape), cmp_pe[l, 0], cmp_w1[l, 0], cmp_b1[l, 0],
                                         cmp_w2[l, 0], cmp_b2[l, 0]), k_norm[l, 0])
        v_cmp = compress_blocks(vc.reshape(kv_shape), cmp_pe[l, 1], cmp_w1[l, 1], cmp_b1[l, 1],
                                cmp_w2[l, 1], cmp_b2[l, 1])
        k_sel = rms_norm(ksl.reshape(kv_shape), k_norm[l, 1])
        k_win = rms_norm(kwn.reshape(kv_shape), k_norm[l, 2])
        nsa_gates = jax.nn.sigmoid(nsa_g).reshape(b, s, NSA_KV_HEADS, NSA_GROUP, N_NSA_BRANCHES)
        y_nsa = native_sparse_attention(qh, k_cmp, v_cmp, k_sel, vsl.reshape(kv_shape),
                                        k_win, vwn.reshape(kv_shape), nsa_gates)

        y_sc = sc_b * causal_depthwise_conv(sc_c * sc_h, sc_conv_w[l])

        gates = jax.nn.sigmoid(merge_g).reshape(b, s, N_MIXERS, D_MODEL)
        merged = (gates[:, :, 0] * (y_rnn @ w_rnn_out[l])
                  + gates[:, :, 1] * (y_nsa @ w_nsa_out[l])
                  + gates[:, :, 2] * (y_sc @ w_sc_out[l]))
        x = x + merged @ w_out[l]

        x = x + hierarchical_moe(rms_norm(x, ffn_norm[l]), router_group_w[l], router_group_b[l],
                                 router_expert_w[l], router_expert_b[l],
                                 exp_w_gate[l], exp_w_up[l], exp_w_down[l])
    return x


_drawn_inputs = setup_inputs


def setup_inputs(seed=0):
    import zlib

    import numpy as np

    out = dict(_drawn_inputs(seed))
    spreads = {}
    factors = {'rg_ba': 38.138,
     'rg_bx': 34.564,
     'cmp_b1': 8.0,
     'cmp_b2': 8.0,
     'q_norm': 5.266,
     'k_norm': 5.487,
     'router_group_b': 8.0,
     'router_expert_b': 3.363,
     'rnn_conv_b': 3.303}
    for name, (base, spread) in spreads.items():
        noise = np.random.default_rng([zlib.crc32(name.encode()), seed]).standard_normal(out[name].shape)
        drawn = base * np.exp(spread * noise) if base else spread * noise
        out[name] = __import__('jax').numpy.asarray(drawn.astype(out[name].dtype))
    for name, factor in factors.items():
        out[name] = (out[name] * factor).astype(out[name].dtype)
    return out
```

```python
from contextlib import ExitStack

import numpy as np

import concourse.bass as bass
from concourse import mybir

fp32 = mybir.dt.float32
i32 = mybir.dt.int32
ALU = mybir.AluOpType
ACT = mybir.ActivationFunctionType
AX = mybir.AxisListType

P = 128
S, D = 256, 1024
TT = S // P
KD = D // P
W4 = 512
CT = W4 // P
HD = 64
HEADS, GROUPS = 8, 2
HG = HEADS // GROUPS
NCMP, CL, CS = 15, 32, 16
LP = CL // 2
RNN_TAPS, SC_TAPS = 4, 3
NEG = -1e30
EPS = 1e-6
E, EG = 32, 4
NG = E // EG
F = 256
SLOTS = 32
MAXR = S // SLOTS
RING = 6
SLOT = 4096
CB = 512

C_RX, C_RY, C_Q, C_KC, C_KSL, C_KWN, C_SB, C_SC, C_SH, C_MG = (
    0, 512, 1024, 1536, 1792, 2048, 2328, 2840, 3352, 3864)
KVA = C_KWN - C_KC
KVB = C_SB - C_KWN
BR = (0, 2, 1)

LOADS = (["q", "kva", "kvb", "rx", "cmp", "ry", "sb", "sc", "sh"]
         + [f"{x}{b}" for b in BR for x in ("ga", "gb", "w")] + ["wo0", "wo1"])
LI = {n: i for i, n in enumerate(LOADS)}
UNITS = [(0, 0), (1, 0), (0, 1), (1, 1)]


def fills_of_unit(u):
    tt = UNITS[u][1]
    return [f"pt{u}_{br}{sb}" for br in range(2) for sb in range(tt + 1)] + [f"ptc{u}", f"o{u}"]


FILLS = (["par"] + [f"xT{i}" for i in range(4)] + ["q0", "q1", "kvs", "kc", "vc", "kvw0", "kvw1", "rx0", "rx1",
         "qT0", "qT1", "kTs", "kTw", "hid", "ry0", "ry1", "cmp2", "r0", "r1", "i0", "i1", "kcT",
         "sb0", "sb1", "Sc0", "Sc1", "sc0", "sc1"] + fills_of_unit(0) + ["sh0", "sh1"] + fills_of_unit(1)
         + ["ga0_0", "ga0_1"] + fills_of_unit(2) + ["gb0_0", "gb0_1"] + fills_of_unit(3)
         + [f"p0_{i}" for i in range(4)]
         + [f"{x}{b}_{i}" for b in BR[1:] for x, m in (("ga", 2), ("gb", 2), ("p", 4)) for i in range(m)]
         + [f"mT{i}" for i in range(4)] + [f"wo{i}" for i in range(4)]
         + ["x2T0", "x2T1", "rl0", "x2T2", "x2T3", "rl1", "pos"])
FI = {n: i for i, n in enumerate(FILLS)}
LAST_USE = {"q": "q1", "kva": "vc", "kvb": "kvw1", "rx": "rx1", "cmp": "hid", "ry": "ry1", "sb": "sb1", "sc": "sc1",
            "sh": "sh1", "wo0": "wo3", "wo1": "wo3"}
for _b in BR:
    LAST_USE.update({f"ga{_b}": f"ga{_b}_1", f"gb{_b}": f"gb{_b}_1", f"w{_b}": f"p{_b}_3"})

ROWS, _at = {}, 0
for _n, _k in (("cw", 16), ("cb", 4), ("sw", 12), ("ba", 4), ("bx", 4), ("lam", 4), ("b1", 2), ("qn", 1),
               ("kn", 3), ("pe", 32)):
    ROWS[_n] = _at
    _at += _k
NROWS = _at
KR = 36


def trunk(nc, x, mix_norm, w_in, rnn_conv_w, rnn_conv_b, rg_wa, rg_ba, rg_wx, rg_bx, rg_lambda,
          cmp_pe, cmp_w1, cmp_b1, cmp_w2, cmp_b2, q_norm, k_norm, sc_conv_w,
          w_rnn_out, w_nsa_out, w_sc_out, w_out, ffn_norm,
          router_group_w, router_group_b, router_expert_w, router_expert_b,
          exp_w_gate, exp_w_up, exp_w_down, out):
    ctx = ExitStack()
    with ctx:
        def sb(name, shape, dt=fp32):
            return ctx.enter_context(nc.sbuf_tensor(name, shape, dt))

        def sem(name):
            return ctx.enter_context(nc.semaphore(name))

        ring = sb("ring", [P, RING, SLOT])
        xT = sb("xT", [P, KD, S])
        tok = sb("tok", [P, TT, D])
        yT = sb("yT", [P, 3, CT, S])
        gate = sb("gate", [P, 4, CB])
        pcol = sb("pcol", [P, NROWS])
        ident = sb("ident", [P, P])
        tri = sb("tri", [P, P])
        ones = sb("ones", [P, P])
        cmask = sb("cmask", [P, 2 * P])
        nmask = sb("nmask", [P, TT, NCMP])
        ngany = sb("ngany", [P, TT])
        iot = sb("iot", [P, SLOTS])
        desc = sb("desc", [P, E])
        thr = sb("thr", [P, MAXR])
        wbd = sb("wbd", [P, 2, CT, P])
        w2 = sb("w2", [P, 2, HD])
        b2 = sb("b2", [NCMP, 2, HD])
        rw = sb("rw", [P, KD, KR])
        rb = sb("rb", [P, KR])
        small = sb("small", [P, P])
        nrounds = sb("nrounds", [1, 1], i32)
        a_rnn = sb("a_rnn", [P, 5 * CT * S + 16])
        a_sc = sb("a_sc", [P, 2 * CT * S + 16])
        a_att = sb("a_att", [P, 9216 + 320])

        def part(area, at, shape):
            n = int(np.prod(shape))
            v = area[:, at:at + n]
            names = "abcd"[:len(shape)]
            return v.rearrange(f"p ({' '.join(names)}) -> p {' '.join(names)}", **dict(zip(names, shape)))

        CTS = CT * S
        rxp = part(a_rnn, 0, (CT, S + 4))
        u = part(a_rnn, CTS + 16, (CT, S))
        rg = part(a_rnn, 2 * CTS + 16, (CT, S))
        ig = part(a_rnn, 3 * CTS + 16, (CT, S))
        rr = part(a_rnn, 4 * CTS + 16, (CT, S))
        root = part(a_rnn, 0, (CT, S))
        zp = part(a_sc, 0, (CT, S + 4))
        scc = part(a_sc, CTS + 16, (CT, S))
        q_sb = part(a_att, 0, (TT, W4))
        kvs = part(a_att, 1024, (TT, 256))
        kvw = part(a_att, 1536, (TT, 256))
        qT = part(a_att, 2048, (CT, S))
        kT = part(a_att, 3072, (2, GROUPS, S))
        s_sb = part(a_att, 4096, (2, HG, S))
        pT = part(a_att, 6144, (2, TT, HG, P))
        pTc = part(a_att, 8192, (P,))
        pc = part(a_att, 8320, (TT, HEADS, 32))
        cmpT = part(a_att, 8832, (GROUPS, 16))
        kcd = part(a_att, 8864, (GROUPS, P))
        ngs = part(a_att, 9120, (TT, 24))
        coef = part(a_att, 9168, (4, 16))
        l_sb = part(a_att, 9232, (2, HG))
        nm = part(a_att, 9240, (2, HG))
        ssq = part(a_att, 9248, (TT, 12))
        sq12 = part(a_att, 9280, (TT, 12))
        prow = part(a_att, 4096, (P,))
        kcv = part(a_att, 4096, (2, GROUPS, S))
        sqs = part(a_att, 5120, (TT, W4))
        kd = part(a_att, 5120, (2, TT, GROUPS, P))
        cx = part(a_att, 6144, (2, LP, GROUPS * NCMP))
        hid = part(a_att, 7104, (2, GROUPS * NCMP))
        kc_sb = part(a_att, 7168, (GROUPS, HD))
        kc_sq = part(a_att, 7296, (GROUPS, HD))
        vbd = tok[:, 0, 0:GROUPS * HG * HD].rearrange("p (g h d) -> p g h d", g=GROUPS, h=HG)
        gain = part(a_sc, CTS + 16, (D,))
        x1 = part(a_rnn, 0, (TT, D))
        posx = part(a_att, 0, (TT, MAXR * E + EG))
        combx = part(a_att, 640, (TT, MAXR * E + EG))
        hot = part(a_att, 1280, (TT, EG, SLOTS))
        hotw = part(a_att, 1536, (TT, EG, SLOTS))
        hotT = part(a_att, 1792, (TT, P))
        hs = part(a_att, 2048, (F,))
        h = part(a_att, 2304, (F,))
        hT = part(a_att, 2560, (2, P))
        xg = part(a_att, 4096, (KD, P))
        o_sb = part(a_att, 5120, (D,))
        lg = part(a_att, 6144, (TT, KR))
        rt = part(a_att, 6400, (12, TT, E))
        rs = part(a_att, 7200, (12, TT))
        y_sb = part(a_sc, 0, (TT, D))

        psum = ctx.enter_context(nc.psum_tensor("psum", [P, 8, 512], fp32))

        def bank(n):
            return psum[:, FI[n] % 4, :]

        def bank3(n, a, b):
            return bank(n)[:, 0:a * b].rearrange("p (a b) -> p a b", a=a)

        s_ps = [psum[:, b:b + 2, :].rearrange("p a (h s) -> p h a s", h=2) for b in (4, 6)]
        y_ps = psum[:, 0:4, :]
        xo = psum[:, 4:6, :]
        h_ps = psum[:, 6, :]
        t_ps = psum[:, 7, :]

        slot_full = [sem(f"slot_full{i}") for i in range(RING)]
        bank_full = sem("bank_full")
        bank_free = [sem(f"bank_free{i}") for i in range(4)]
        x_loaded = [sem(f"x_loaded{t}") for t in range(TT)]
        gain_loaded, rows_loaded, small_loaded, x_again = map(sem, (
            "gain_loaded", "rows_loaded", "small_loaded", "x_again"))
        consts, pads = sem("consts"), sem("pads")
        dve_chain, act_chain, pool_chain = sem("dve_chain"), sem("act_chain"), sem("pool_chain")
        x_squares, x_mean, x_root, x_normed = map(sem, ("x_squares", "x_mean", "x_root", "x_normed"))
        qk_mean, qk_root, qk_normed = map(sem, ("qk_mean", "qk_root", "qk_normed"))
        lam_ready, lam_exp, lru_scale = map(sem, ("lam_ready", "lam_exp", "lru_scale"))
        u_ready, r_tanh, th_ready, negth_ready, root_ready = map(sem, (
            "u_ready", "r_tanh", "th_ready", "negth_ready", "root_ready"))
        cx_ready, kc_mean, kc_root, kc_normed = map(sem, ("cx_ready", "kc_mean", "kc_root", "kc_normed"))
        sc_shifted, sc_exped, pc_ready = map(sem, ("sc_shifted", "sc_exped", "pc_ready"))
        scores_full, scores_maxed, scores_exped, probs_ready = map(sem, (
            "scores_full", "scores_maxed", "scores_exped", "probs_ready"))
        y_rnn_ready, y_sc_ready, merged_ready = map(sem, ("y_rnn_ready", "y_sc_ready", "merged_ready"))
        x1_ready, x2_squares, x2_mean, x2_root, x2_normed = map(sem, (
            "x1_ready", "x2_squares", "x2_mean", "x2_root", "x2_normed"))
        g_shifted, g_exped, m_shifted, m_exped, picks_ready, rounds_ready = map(sem, (
            "g_shifted", "g_exped", "m_shifted", "m_exped", "picks_ready", "rounds_ready"))
        kpair_done, down_done, gather_done, hotT_done, hT_done, scatter_done = map(sem, (
            "kpair_done", "down_done", "gather_done", "hotT_done", "hT_done", "scatter_done"))
        hot_ready, hotw_ready, silu_done, h_ready, hT_copied, hotT_copied = map(sem, (
            "hot_ready", "hotw_ready", "silu_done", "h_ready", "hT_copied", "hotT_copied"))
        xg_act, xg_dve, o_act, o_dve, y_ready, stored = map(sem, (
            "xg_act", "xg_dve", "o_act", "o_dve", "y_ready", "stored"))

        def copies(name):
            return 2 if name in ("cmp",) else 1

        def slot_count(name):
            i = LI[name]
            return 16 * sum(copies(LOADS[j]) for j in range(i % RING, i + 1, RING))

        NL = len(LOADS)
        MS = [(NL + j) % RING for j in range(RING)]
        MBASE = [16 * sum(copies(LOADS[j]) for j in range(s, NL, RING)) for s in MS]

        def slot(name):
            return ring[:, LI[name] % RING, :]

        def full(eng, name):
            eng.wait_ge(bank_full, FI[name] + 1)

        def freed(ins, name):
            ins.then_inc(bank_free[FI[name] % 4], 1)

        def bc(ap, shape):
            return ap.to_broadcast(shape)

        block = ctx.enter_context(nc.Block())

        wg_v = exp_w_gate[0].rearrange("(g e) (p k) f -> g p e (k f)", e=EG, p=P)
        wu_v = exp_w_up[0].rearrange("(g e) (p k) f -> g p e (k f)", e=EG, p=P)
        wd_v = exp_w_down[0].rearrange("(g e) (p c) n -> g p e c n", e=EG, p=P)
        win_v = w_in[0].rearrange("(k p) n -> p k n", p=P)

        @block.sync
        def _(sp):
            def columns(name, c0, n):
                dst = slot(name)[:, 0:KD * n].rearrange("p (k n) -> p k n", k=KD)
                sp.dma_start(dst, win_v[:, :, c0:c0 + n]).then_inc(slot_full[LI[name] % RING], 16)

            def whole(name, w):
                dst = slot(name)[:, :].rearrange("p (k n) -> p k n", k=CT)
                sp.dma_start(dst, w[0].rearrange("(k p) n -> p k n", p=P)).then_inc(slot_full[LI[name] % RING], 16)

            def reuse(i):
                if i >= RING:
                    full(sp, LAST_USE[LOADS[i - RING]])

            for i, name in enumerate(LOADS):
                reuse(i)
                if name == "q":
                    columns(name, C_Q, CB)
                elif name == "kva":
                    columns(name, C_KC, KVA)
                elif name == "kvb":
                    columns(name, C_KWN, KVB)
                elif name == "cmp":
                    for kv in range(2):
                        dst = slot(name)[:, kv * LP * P:(kv + 1) * LP * P].rearrange("p (l n) -> p l n", l=LP)
                        sp.dma_start(dst, cmp_w1[0, kv].rearrange("(l p) n -> p l n", p=P)
                                     ).then_inc(slot_full[i % RING], 16)
                elif name in ("rx", "ry", "sb", "sc", "sh"):
                    columns(name, dict(rx=C_RX, ry=C_RY, sb=C_SB, sc=C_SC, sh=C_SH)[name], CB)
                elif name[0] == "g":
                    columns(name, C_MG + int(name[2]) * D + (name[1] == "b") * CB, CB)
                elif name[0:2] == "wo":
                    dst = slot(name)[:, :].rearrange("p (k n) -> p k n", k=KD)
                    sp.dma_start(dst, w_out[0].rearrange("(k p) n -> p k n", p=P)[:, :, int(name[2]) * CB:][:, :, 0:CB]
                                 ).then_inc(slot_full[i % RING], 16)
                else:
                    whole(name, (w_rnn_out, w_nsa_out, w_sc_out)[int(name[1])])

            def experts(g, j):
                s = MS[j]
                if j < 4:
                    dst = ring[:, s, :].rearrange("p (m e n) -> p m e n", m=2, e=EG)
                    for m, w in enumerate((wg_v, wu_v)):
                        src = w[g][:, :, j * 2 * F:(j + 1) * 2 * F] if isinstance(g, int) else \
                            w[bass.ds(g, 1), :, :, j * 2 * F:(j + 1) * 2 * F].rearrange("g p e n -> p (g e) n")
                        sp.dma_start(dst[:, m], src).then_inc(slot_full[s], 16)
                else:
                    dst = ring[:, s, :].rearrange("p (e c n) -> p e c n", e=EG, c=2)
                    for c in range(2):
                        lo = (j - 4) * CB
                        src = wd_v[g][:, :, c, lo:lo + CB] if isinstance(g, int) else \
                            wd_v[bass.ds(g, 1), :, :, c, lo:lo + CB].rearrange("g p e n -> p (g e) n")
                        sp.dma_start(dst[:, :, c, :], src).then_inc(slot_full[s], 16)

            for j in range(6):
                reuse(NL + j)
                experts(0, j)

            def regroup(g, it):
                for j in range(6):
                    if j < 4:
                        sp.wait_ge(kpair_done, it * 4 + (j - 3))
                    else:
                        sp.wait_ge(down_done, it * 2 + (j - 5))
                    experts(g, j)

            with sp.Fori(1, NG) as g:
                regroup(g, g)
            sp.wait_ge(rounds_ready, 1)
            nr = sp.value_load(nrounds[0:1, 0:1], min_val=1, max_val=MAXR)
            with sp.If(nr > 1):
                with sp.Fori(1, nr) as r:
                    with sp.Fori(0, NG) as g:
                        regroup(g, r * NG + g)
            sp.end_ifs()
            for i in range(4):
                sp.wait_ge(y_ready, i + 1)
                t, hf = i // 2, i % 2
                sp.dma_start(out[0, t * P:(t + 1) * P, hf * CB:(hf + 1) * CB], y_sb[:, t, hf * CB:(hf + 1) * CB]
                             ).then_inc(stored, 16)
            sp.wait_ge(stored, 64)

        @block.gpsimd
        def _(pool):
            g = nc.gpsimd
            n = [0]

            def step(ins):
                n[0] += 1
                ins.then_inc(pool_chain, 1)

            def settle():
                pool.wait_ge(pool_chain, n[0])

            step(g.memset(prow[:], 0.0))
            step(g.memset(ident[:], 0.0))
            step(g.memset(tri[:], 1.0))
            step(g.memset(cmask[:], 0.0))
            step(g.memset(nmask[:], 0.0))
            step(g.memset(ngany[:], 1.0))
            settle()
            def rows(name, src, c0=0, c1=P):
                r = ROWS[name]
                g.dma_start(prow[r:r + src.shape[0], c0:c1], src).then_inc(rows_loaded, 16)
            rows("cw", rnn_conv_w[0].rearrange("a (c p) -> (a c) p", p=P))
            rows("cb", rnn_conv_b.rearrange("a (c p) -> (a c) p", p=P))
            rows("sw", sc_conv_w[0].rearrange("a (c p) -> (a c) p", p=P))
            rows("ba", rg_ba[0].rearrange("(c h) i -> c (h i)", h=2))
            rows("bx", rg_bx[0].rearrange("(c h) i -> c (h i)", h=2))
            rows("lam", rg_lambda.rearrange("a (c p) -> (a c) p", p=P))
            rows("b1", cmp_b1[0])
            for c in (0, HD):
                rows("qn", q_norm, c, c + HD)
                rows("kn", k_norm[0], c, c + HD)
            rows("pe", cmp_pe[0].rearrange("v (l j) d -> (v l) (j d)", j=2))
            step(g.affine_select(out=ident[:], in_=ident[:], compare_op=ALU.not_equal, fill=1.0, base=0,
                                 pattern=[[-1, P]], channel_multiplier=1))
            step(g.affine_select(out=cmask[:, P:], in_=cmask[:, P:], compare_op=ALU.is_ge, fill=NEG, base=0,
                                 pattern=[[-1, P]], channel_multiplier=1))
            step(g.affine_select(out=nmask[:], in_=nmask[:], compare_op=ALU.is_ge, fill=NEG, base=1 - CL,
                                 pattern=[[P, TT], [-CS, NCMP]], channel_multiplier=1))
            step(g.affine_select(out=ngany[:], in_=ngany[:], compare_op=ALU.is_ge, fill=0.0, base=1 - CL,
                                 pattern=[[P, TT]], channel_multiplier=1))
            step(g.affine_select(out=tri[:], in_=tri[:], compare_op=ALU.is_gt, fill=0.0, base=0,
                                 pattern=[[1, P]], channel_multiplier=-1))
            step(g.memset(ones[:], 1.0))
            step(g.iota(iot[:], pattern=[[1, SLOTS]], base=0, channel_multiplier=0, allow_small_or_imprecise_dtypes=True))
            step(g.iota(desc[:], pattern=[[-1, E]], base=E, channel_multiplier=0, allow_small_or_imprecise_dtypes=True))
            step(g.iota(thr[:], pattern=[[SLOTS, MAXR]], base=0, channel_multiplier=0, allow_small_or_imprecise_dtypes=True))
            settle()
            g.memset(rxp[:, :, 0:3], 0.0).then_inc(consts, 1)
            step(g.memset(wbd[:], 0.0))
            settle()
            for i, w in enumerate((rg_wa, rg_wx)):
                for hh in range(2):
                    g.dma_start(wbd[hh * HD:(hh + 1) * HD, i, :, hh * HD:(hh + 1) * HD],
                                w[0].rearrange("(c h) i j -> h i c j", h=2)[hh]).then_inc(small_loaded, 16)
            g.dma_start(w2[:], cmp_w2[0].rearrange("v p d -> p v d")).then_inc(small_loaded, 16)
            g.dma_start(b2[:], cmp_b2[0].partition_broadcast(NCMP)).then_inc(small_loaded, 16)
            g.dma_start(rw[:, :, 0:4], router_group_w[0].rearrange("(p k) e -> p k e", p=P)).then_inc(small_loaded, 16)
            g.dma_start(rw[:, :, 4:KR], router_expert_w[0].rearrange("(p k) e -> p k e", p=P)).then_inc(small_loaded, 16)
            g.dma_start(rb[:, 0:4], router_group_b[0].partition_broadcast(P)).then_inc(small_loaded, 16)
            g.dma_start(rb[:, 4:KR], router_expert_b[0].partition_broadcast(P)).then_inc(small_loaded, 16)
            g.memset(zp[:, :, 0:2], 0.0).then_inc(pads, 1)
            full(pool, "xT3")
            g.memset(vbd[:], 0.0).then_inc(pads, 1)
            g.memset(pc[:], 0.0).then_inc(pads, 1)
        N_ROWDMA, N_SMALLDMA = 12, 10

        @block.scalar
        def _(act):
            a = nc.scalar
            for t in range(TT):
                act.dma_start(tok[:, t, :], x[0, t * P:(t + 1) * P, :]).then_inc(x_loaded[t], 16)
            act.dma_start(gain[:], mix_norm[0].partition_broadcast(P)).then_inc(gain_loaded, 16)
            for t in range(TT):
                act.wait_ge(x_loaded[t], 16)
                a.activation(xT[:, 4 * t:4 * t + 4, :].rearrange("p k s -> p (k s)"), tok[:, t, :], ACT.Square,
                             accum_out=small[:, t:t + 1]).then_inc(x_squares, 1)
            act.wait_ge(x_mean, 1)
            a.activation(small[:, 4:6], small[:, 2:4], ACT.Sqrt).then_inc(x_root, 1)
            act.wait_ge(lam_ready, 1)
            a.activation(small[:, 24:28], small[:, 20:24], ACT.Exp).then_inc(lam_exp, 1)
            for i in (0, 2):
                full(act, f"xT{i}")
                freed(a.copy(xT[:, 4 * (i % 2):4 * (i % 2) + 4, (i // 2) * P:(i // 2 + 1) * P],
                             bank3(f"xT{i}", 4, P)), f"xT{i}")
            for t in range(TT):
                full(act, f"q{t}")
                freed(a.copy(q_sb[:, t, :], bank(f"q{t}")), f"q{t}")
            full(act, "kvs")
            freed(a.copy(kvs[:], bank3("kvs", 2, 256)), "kvs")
            for i, name in enumerate(("kc", "vc")):
                full(act, name)
                freed(a.copy(kcv[:, i], bank3(name, 2, S)), name)
            for t in range(TT):
                name = f"kvw{t}"
                full(act, name)
                a.activation(ngs[:, t, :], bank(name)[:, 256:280], ACT.Tanh, scale=0.5)
                freed(a.copy(kvw[:, t, :], bank(name)[:, 0:256]), name)
            act.wait_ge(consts, 1)
            for i in range(2):
                full(act, f"rx{i}")
                freed(a.copy(rxp[:, 2 * i:2 * i + 2, 3:3 + S], bank3(f"rx{i}", 2, S)), f"rx{i}")
            act.wait_ge(qk_mean, 1)
            a.activation(sq12[:], ssq[:], ACT.Sqrt).then_inc(qk_root, 1)
            full(act, "hid")
            for kv in range(2):
                ins = a.activation(hid[:, kv, :], bank("hid")[:, kv * 32:kv * 32 + 30], ACT.Gelu_apprx_tanh,
                                   bias=pcol[:, ROWS["b1"] + kv:ROWS["b1"] + kv + 1])
            freed(ins, "hid")
            for i in range(2):
                full(act, f"ry{i}")
                freed(a.activation(yT[:, 0, 2 * i:2 * i + 2, :], bank3(f"ry{i}", 2, S), ACT.Gelu_apprx_tanh), f"ry{i}")
            act.wait_ge(kc_mean, 1)
            a.activation(small[0:NCMP, 70:72], small[0:NCMP, 68:70], ACT.Sqrt).then_inc(kc_root, 1)
            act.wait_ge(lru_scale, 1)
            for gname, dst, col in (("r", rg, 40), ("i", ig, 44)):
                for i in range(2):
                    name = f"{gname}{i}"
                    full(act, name)
                    for c in range(2):
                        ct = 2 * i + c
                        ins = a.activation(dst[:, ct, :], bank3(name, 2, S)[:, c, :], ACT.Tanh, scale=0.5,
                                           bias=small[:, col + ct:col + ct + 1])
                    freed(ins, name)
            act.wait_ge(bank_free[FI["r1"] % 4], FI["r1"] // 4 + 1)
            for ct in range(CT):
                ins = a.activation(rg[:, ct, :], rg[:, ct, :], ACT.Tanh, scale=small[:, 48 + ct:49 + ct],
                                   bias=small[:, 48 + ct:49 + ct])
            ins.then_inc(th_ready, 1)
            act.wait_ge(negth_ready, 1)
            a.activation(root[:], rg[:], ACT.Sqrt).then_inc(root_ready, 1)

            for i in range(2):
                full(act, f"sb{i}")
                freed(a.copy(yT[:, 2, 2 * i:2 * i + 2, :], bank3(f"sb{i}", 2, S)), f"sb{i}")

            def exps(n):
                tt = UNITS[n][1]
                w = P * (tt + 1)
                for br in range(2):
                    act.wait_ge(scores_maxed, 2 * n + br + 1)
                    for hh in range(HG):
                        ins = a.activation(s_sb[:, br, hh, 0:w], s_sb[:, br, hh, 0:w], ACT.Exp,
                                           bias=nm[:, br, hh:hh + 1], accum_out=l_sb[:, br, hh:hh + 1])
                    ins.then_inc(scores_exped, 1)

            def turned(n):
                tt = UNITS[n][1]
                for sbk in range(tt + 1):
                    name = f"pt{n}_0{sbk}"
                    full(act, name)
                    freed(a.copy(pT[:, 0, sbk], bank3(name, HG, P)), name)
                full(act, f"ptc{n}")
                freed(a.copy(pTc[:], bank(f"ptc{n}")[:, 0:P]), f"ptc{n}")

            def output(n):
                g, tt = UNITS[n]
                full(act, f"o{n}")
                freed(a.copy(yT[:, 1, 2 * g:2 * g + 2, tt * P:(tt + 1) * P], bank3(f"o{n}", 2, P)), f"o{n}")

            exps(0)
            act.wait_ge(sc_shifted, 1)
            a.activation(pc[:, :, :, 0:NCMP], pc[:, :, :, 0:NCMP], ACT.Exp).then_inc(sc_exped, 1)
            for i in range(2):
                full(act, f"sc{i}")
                freed(a.copy(scc[:, 2 * i:2 * i + 2, :], bank3(f"sc{i}", 2, S)), f"sc{i}")

            def gates(b, half):
                if b != BR[0]:
                    last = f"p{BR[BR.index(b) - 1]}_{2 * half + 1}"
                    act.wait_ge(bank_free[FI[last] % 4], FI[last] // 4 + 1)
                for t in range(TT):
                    name = f"g{'ab'[half]}{b}_{t}"
                    full(act, name)
                    freed(a.activation(gate[:, 2 * half + t, :], bank(name), ACT.Tanh, scale=0.5), name)

            turned(0)
            output(0)
            exps(1)
            turned(1)
            output(1)
            exps(2)
            gates(0, 0)
            turned(2)
            output(2)
            exps(3)
            gates(0, 1)
            turned(3)
            output(3)
            act.wait_ge(y_rnn_ready, 1)
            act.wait_ge(y_sc_ready, 1)
            act.dma_start(x1[:], x[0].rearrange("(t p) n -> p t n", p=P)).then_inc(x_again, 16)
            act.dma_start(gain[:], ffn_norm[0].partition_broadcast(P)).then_inc(x_again, 16)
            for b in BR[1:]:
                for half in range(2):
                    gates(b, half)
            for i in (0, 2):
                full(act, f"mT{i}")
                freed(a.mul(xT[:, 4 * (i % 2):4 * (i % 2) + 4, (i // 2) * P:(i // 2 + 1) * P],
                            bank3(f"mT{i}", 4, P), 0.5), f"mT{i}")
            for t in range(TT):
                act.wait_ge(x1_ready, t + 1)
                a.activation(tok[:, t, :], x1[:, t, :], ACT.Square, accum_out=small[:, 80 + t:81 + t]
                             ).then_inc(x2_squares, 1)
                act.wait_ge(x2_mean, t + 1)
                a.activation(small[:, 84 + t:85 + t], small[:, 82 + t:83 + t], ACT.Sqrt).then_inc(x2_root, 1)
            for t in range(TT):
                full(act, f"x2T{2 * t}")
                freed(a.copy(xT[:, 0:4, t * P:(t + 1) * P], bank3(f"x2T{2 * t}", 4, P)), f"x2T{2 * t}")
            act.wait_ge(g_shifted, 1)
            a.activation(rt[:, 1, :, 0:4], rt[:, 0, :, 0:4], ACT.Exp).then_inc(g_exped, 1)
            act.wait_ge(m_shifted, 1)
            a.activation(rs[:, 8, :], rs[:, 7, :], ACT.Exp).then_inc(m_exped, 1)

            act.wait_ge(gather_done, 1)
            a.copy(xg[:, 0:4, :], xo[:, 0, :].rearrange("p (k s) -> p k s", k=4)).then_inc(xg_act, 1)
            act.wait_ge(rounds_ready, 1)
            nr = act.value_load(nrounds[0:1, 0:1], min_val=1, max_val=MAXR)
            with act.Fori(0, nr * NG) as it:
                act.wait_ge(kpair_done, it * 4 + 4)
                a.activation(hs[:], h_ps[:, 0:F], ACT.Silu).then_inc(silu_done, 1)
                act.wait_ge(gather_done, it * 2 + 3)
                a.copy(xg[:, 0:4, :], xo[:, 0, :].rearrange("p (k s) -> p k s", k=4)).then_inc(xg_act, 1)
                act.wait_ge(hT_done, it + 1)
                a.copy(hT[:], t_ps[:, 0:2 * P].rearrange("p (c s) -> p c s", c=2)).then_inc(hT_copied, 1)
                act.wait_ge(down_done, it * 2 + 1)
                a.copy(o_sb[:, 0:CB], xo[:, 0, :]).then_inc(o_act, 1)

        @block.vector
        def _(dve):
            v = nc.vector
            n = [0]
            last = [None]

            def do(ins):
                n[0] += 1
                ins.then_inc(dve_chain, 1)
                last[0] = (dve_chain, n[0])

            def signal(ins, s, value):
                ins.then_inc(s, 1)
                last[0] = (s, value)

            def free(ins, name):
                freed(ins, name)
                last[0] = (bank_free[FI[name] % 4], FI[name] // 4 + 1)

            def settle():
                dve.wait_ge(*last[0])

            def chain(ins):
                do(ins)
                settle()

            def col(name, i=0, rows=slice(0, P)):
                return pcol[rows, ROWS[name] + i:ROWS[name] + i + 1]

            full(dve, "par")
            free(v.tensor_copy(pcol[:], bank("par")[:, 0:NROWS]), "par")
            dve.wait_ge(x_squares, 2)
            signal(v.tensor_scalar(small[:, 2:4], small[:, 0:2], 1.0 / D, EPS, ALU.mult, ALU.add), x_mean, 1)
            settle()
            lam = pcol[:, ROWS["lam"]:ROWS["lam"] + CT]
            chain(v.tensor_scalar(small[:, 16:20], lam, -1.0, None, ALU.mult))
            signal(v.tensor_tensor(small[:, 20:24], small[:, 16:20], lam, ALU.min), lam_ready, 1)
            do(v.tensor_scalar(small[:, 40:44], pcol[:, ROWS["ba"]:ROWS["ba"] + CT], 0.5, None, ALU.mult))
            do(v.tensor_scalar(small[:, 44:48], pcol[:, ROWS["bx"]:ROWS["bx"] + CT], 0.5, None, ALU.mult))
            do(v.tensor_scalar(small[:, 60:61], col("qn"), HD ** -0.5, None, ALU.mult))
            dve.wait_ge(x_root, 1)
            chain(v.reciprocal(small[:, 6:8], small[:, 4:6]))
            dve.wait_ge(gain_loaded, 16)
            for t in range(TT):
                signal(v.scalar_tensor_tensor(tok[:, t, :], tok[:, t, :], small[:, 6 + t:7 + t], gain[:],
                                              ALU.mult, ALU.mult), x_normed, t + 1)
            dve.wait_ge(lam_exp, 1)
            z, w, w2_, acc = (small[:, c:c + CT] for c in (24, 28, 32, 36))
            chain(v.tensor_scalar(w, z, 2.0, None, ALU.add))
            chain(v.reciprocal(w, w))
            chain(v.tensor_tensor(w, w, z, ALU.mult))
            chain(v.tensor_tensor(w2_, w, w, ALU.mult))
            chain(v.tensor_scalar(acc, w2_, 1.0 / 17, None, ALU.mult))
            for k in (15, 13, 11, 9, 7, 5, 3):
                chain(v.scalar_tensor_tensor(acc, acc, 1.0 / k, w2_, ALU.add, ALU.mult))
            chain(v.scalar_tensor_tensor(acc, acc, 1.0, w, ALU.add, ALU.mult))
            chain(v.tensor_scalar(small[:, 16:20], small[:, 16:20], 0.0, -2.0, ALU.max, ALU.mult))
            signal(v.scalar_tensor_tensor(small[:, 48:52], acc, -4.0, small[:, 16:20], ALU.mult, ALU.add), lru_scale, 1)
            for i in (1, 3):
                full(dve, f"xT{i}")
                free(v.tensor_copy(xT[:, 4 * (i % 2):4 * (i % 2) + 4, (i // 2) * P:(i // 2 + 1) * P],
                                   bank3(f"xT{i}", 4, P)), f"xT{i}")

            def wait_freed(eng, name):
                eng.wait_ge(bank_free[FI[name] % 4], FI[name] // 4 + 1)

            wait_freed(dve, "q1")
            heads = q_sb[:].rearrange("p t (h d) -> p (t h) d", d=HD)
            chain(v.tensor_tensor(sqs[:], q_sb[:], q_sb[:], ALU.mult))
            chain(v.tensor_reduce(ssq[:, :, 0:8], sqs[:].rearrange("p t (h d) -> p t h d", d=HD), AX.X, ALU.add))
            wait_freed(dve, "kvw1")
            for i, kk in enumerate((kvs, kvw)):
                chain(v.tensor_tensor(sqs[:, :, 0:P], kk[:, :, 0:P], kk[:, :, 0:P], ALU.mult))
                chain(v.tensor_reduce(ssq[:, :, 8 + 2 * i:10 + 2 * i],
                                      sqs[:, :, 0:P].rearrange("p t (h d) -> p t h d", d=HD), AX.X, ALU.add))
            signal(v.tensor_scalar(ssq[:], ssq[:], 1.0 / HD, EPS, ALU.mult, ALU.add), qk_mean, 1)
            chain(v.tensor_scalar(ngs[:], ngs[:], 0.5, 0.5, ALU.mult, ALU.add))
            for kv in range(2):
                for j in range(2):
                    r = slice(j * HD, (j + 1) * HD)
                    for hi in range(2):
                        src = kcv[r, kv].rearrange("p g (m l j) -> p j l g m", m=CS, j=2)[:, j, :, :, hi:hi + NCMP]
                        lo = hi * 8
                        pe = pcol[r, ROWS["pe"] + kv * LP + lo:ROWS["pe"] + kv * LP + lo + 8]
                        ins = v.tensor_tensor(
                            cx[r, kv, lo:lo + 8, :].rearrange("p l (g n) -> p l g n", g=GROUPS), src,
                            bc(pe.unsqueeze(2).unsqueeze(3), [HD, 8, GROUPS, NCMP]), ALU.add)
                        if kv == 1 and j == 1 and hi == 1:
                            signal(ins, cx_ready, 1)
                        else:
                            do(ins)
            dve.wait_ge(qk_root, 1)
            chain(v.reciprocal(sq12[:], sq12[:]))
            hv = q_sb[:].rearrange("p t (h d) -> p t h d", d=HD)
            do(v.tensor_tensor(hv, hv, bc(sq12[:, :, 0:HEADS].unsqueeze(3), [P, TT, HEADS, HD]), ALU.mult))
            for br, kk in enumerate((kvs, kvw)):
                for j in range(2):
                    c = HEADS + 2 * br
                    ins = v.tensor_tensor(kd[:, br, :, :, j * HD:(j + 1) * HD],
                                          kk[:, :, 0:P].rearrange("p t (g d) -> p t g d", d=HD),
                                          bc(sq12[:, :, c:c + 2].unsqueeze(3), [P, TT, GROUPS, HD]), ALU.mult)
                    if br == 1 and j == 1:
                        signal(ins, qk_normed, 1)
                    else:
                        do(ins)
            for t in range(TT):
                full(dve, f"qT{t}")
                free(v.tensor_scalar(qT[:, :, t * P:(t + 1) * P], bank3(f"qT{t}", CT, P), small[:, 60:61], None,
                                     ALU.mult), f"qT{t}")
            for i, name in enumerate(("kTs", "kTw")):
                full(dve, name)
                free(v.tensor_scalar(kT[:, i], bank3(name, GROUPS, S), col("kn", 1 + i), None, ALU.mult), name)
            wait_freed(dve, "rx1")
            for k in range(RNN_TAPS):
                for ct in range(CT):
                    src = rxp[:, ct, k:k + S]
                    wk = col("cw", k * CT + ct)
                    if k == 0:
                        ins = v.tensor_scalar(u[:, ct, :], src, wk, col("cb", ct), ALU.mult, ALU.add)
                    else:
                        ins = v.scalar_tensor_tensor(u[:, ct, :], src, wk, u[:, ct, :], ALU.mult, ALU.add)
                    if k == RNN_TAPS - 1 and ct == CT - 1:
                        signal(ins, u_ready, 1)
                    else:
                        do(ins)
                settle()

            def maxima(n):
                tt = UNITS[n][1]
                w = P * (tt + 1)
                for br in range(2):
                    dve.wait_ge(scores_full, 2 * n + br + 1)
                    if n:
                        full(dve, f"ptc{n - 1}")
                    chain(v.tensor_tensor(s_sb[:, br].rearrange("p (h a) s -> p h a s", a=2)[:, :, :, 0:w],
                                          s_ps[br][:, :, :, 0:w],
                                          bc(cmask[:, 2 * P - w:2 * P].unsqueeze(1).unsqueeze(1), [P, 2, 2, w]), ALU.add))
                    signal(v.tensor_reduce(nm[:, br, :], s_sb[:, br, :, 0:w], AX.X, ALU.max, negate=True),
                           scores_maxed, 2 * n + br + 1)

            def probs(n):
                g, tt = UNITS[n]
                w = P * (tt + 1)
                for br in range(2):
                    dve.wait_ge(scores_exped, 2 * n + br + 1)
                    chain(v.reciprocal(l_sb[:, br, :], l_sb[:, br, :]))
                    gb = ngs[:, tt, :].rearrange("p (h b) -> p h b", b=3)[:, g * HG:(g + 1) * HG, br + 1]
                    chain(v.tensor_tensor(l_sb[:, br, :], l_sb[:, br, :], gb, ALU.mult))
                    signal(v.tensor_tensor(s_sb[:, br, :, 0:w], s_sb[:, br, :, 0:w],
                                           bc(l_sb[:, br, :].unsqueeze(2), [P, HG, w]), ALU.mult),
                           probs_ready, 2 * n + br + 1)

            def turned(n):
                tt = UNITS[n][1]
                for sbk in range(tt + 1):
                    name = f"pt{n}_1{sbk}"
                    full(dve, name)
                    free(v.tensor_copy(pT[:, 1, sbk], bank3(name, HG, P)), name)

            dve.wait_ge(small_loaded, 16 * N_SMALLDMA)
            dve.wait_ge(pads, 3)
            full(dve, "cmp2")
            kv2 = bank("cmp2")[0:NCMP, 0:256].rearrange("p (v g d) -> p v g d", v=2, g=GROUPS)
            kc = kc_sb[0:NCMP]
            do(v.tensor_tensor(kc, kv2[:, 0], bc(b2[:, 0, :].unsqueeze(1), [NCMP, GROUPS, HD]), ALU.add))
            for hh in range(HG):
                ins = v.tensor_tensor(vbd[32 * hh:32 * hh + NCMP, :, hh, :], kv2[:, 1],
                                      bc(b2[:, 1, :].unsqueeze(1), [NCMP, GROUPS, HD]), ALU.add)
                if hh < HG - 1:
                    do(ins)
                else:
                    free(ins, "cmp2")
            settle()
            chain(v.tensor_tensor(kc_sq[0:NCMP], kc, kc, ALU.mult))
            chain(v.tensor_reduce(small[0:NCMP, 64:66], kc_sq[0:NCMP], AX.X, ALU.add))
            signal(v.tensor_scalar(small[0:NCMP, 68:70], small[0:NCMP, 64:66], 1.0 / HD, EPS, ALU.mult, ALU.add),
                   kc_mean, 1)
            maxima(0)
            dve.wait_ge(kc_root, 1)
            chain(v.reciprocal(small[0:NCMP, 72:74], small[0:NCMP, 70:72]))
            for j in range(2):
                ins = v.tensor_tensor(kcd[0:NCMP, :, j * HD:(j + 1) * HD], kc,
                                      bc(small[0:NCMP, 72:74].unsqueeze(2), [NCMP, GROUPS, HD]), ALU.mult)
                if j == 0:
                    do(ins)
                else:
                    signal(ins, kc_normed, 1)
            full(dve, "kcT")
            free(v.tensor_scalar(cmpT[:, :, 0:NCMP], bank("kcT")[:, 0:32].rearrange("p (g n) -> p g n", g=2)[:, :, 0:NCMP],
                                 col("kn", 0), None, ALU.mult), "kcT")
            dve.wait_ge(th_ready, 1)
            signal(v.tensor_scalar(rg[:], rg[:], -1.0, 1e-30, ALU.mult, ALU.max), negth_ready, 1)
            settle()
            chain(v.tensor_scalar(rr[:], rg[:], 1.0, None, ALU.add))
            chain(v.reciprocal(rr[:], rr[:]))
            wait_freed(dve, "i1")
            do(v.scalar_tensor_tensor(u[:], ig[:], 1.0, u[:], ALU.add, ALU.mult))
            dve.wait_ge(root_ready, 1)
            do(v.scalar_tensor_tensor(rg[:], rg[:], 1.0, rr[:], ALU.subtract, ALU.mult, reverse0=True))
            settle()
            chain(v.tensor_tensor(u[:], u[:], rr[:], ALU.mult))
            chain(v.tensor_tensor(u[:], u[:], root[:], ALU.mult))
            for ct in range(CT):
                do(v.tensor_tensor_scan(rr[:, ct, :], rg[:, ct, :], u[:, ct, :], 0.0, ALU.mult, ALU.add))
            settle()
            wait_freed(dve, "ry1")
            signal(v.tensor_tensor(yT[:, 0], yT[:, 0], rr[:], ALU.mult), y_rnn_ready, 1)
            probs(0)
            pcv = pc[:, :, :, 0:NCMP]
            for a in range(2):
                name = f"Sc{a}"
                full(dve, name)
                scp = bank(name)[:, 0:TT * HEADS * 8].rearrange("p (t h n) -> p t h n", t=TT, h=HEADS // 2)
                for t in range(TT):
                    ins = v.tensor_tensor(pc[:, t].rearrange("p (h a) n -> p h a n", a=2)[:, :, a, 0:NCMP],
                                          scp[:, t, :, 0:NCMP],
                                          bc(nmask[:, t, :].unsqueeze(1), [P, HEADS // 2, NCMP]), ALU.add)
                    if t == 0:
                        do(ins)
                    else:
                        free(ins, name)
            settle()
            c0, c1 = coef[:, 0, :].rearrange("p (t h) -> p t h", t=TT), coef[:, 1, :].rearrange("p (t h) -> p t h", t=TT)
            chain(v.tensor_reduce(c0, pcv, AX.X, ALU.max))
            signal(v.tensor_tensor(pcv, pcv, bc(c0.unsqueeze(3), [P, TT, HEADS, NCMP]), ALU.subtract), sc_shifted, 1)
            dve.wait_ge(sc_exped, 1)
            chain(v.tensor_reduce(c0, pcv, AX.X, ALU.add))
            chain(v.reciprocal(c0, c0))
            chain(v.tensor_tensor(c1, ngs[:].rearrange("p t (h b) -> p t h b", b=3)[:, :, :, 0],
                                  bc(ngany[:].unsqueeze(2), [P, TT, HEADS]), ALU.mult))
            chain(v.tensor_tensor(c0, c0, c1, ALU.mult))
            signal(v.tensor_tensor(pcv, pcv, bc(c0.unsqueeze(3), [P, TT, HEADS, NCMP]), ALU.mult), pc_ready, 1)
            turned(0)
            maxima(1)
            wait_freed(dve, "sc1")
            for i in range(2):
                full(dve, f"sh{i}")
                free(v.tensor_tensor(zp[:, 2 * i:2 * i + 2, 2:2 + S], bank3(f"sh{i}", 2, S),
                                     scc[:, 2 * i:2 * i + 2, :], ALU.mult), f"sh{i}")
            probs(1)
            turned(1)
            maxima(2)
            for k in range(SC_TAPS):
                for ct in range(CT):
                    src = zp[:, ct, k:k + S]
                    wk = col("sw", k * CT + ct)
                    if k == 0:
                        do(v.tensor_scalar(scc[:, ct, :], src, wk, None, ALU.mult))
                    else:
                        do(v.scalar_tensor_tensor(scc[:, ct, :], src, wk, scc[:, ct, :], ALU.mult, ALU.add))
                settle()
            wait_freed(dve, "sb1")
            signal(v.tensor_tensor(yT[:, 2], yT[:, 2], scc[:], ALU.mult), y_sc_ready, 1)
            probs(2)
            turned(2)
            maxima(3)
            probs(3)
            turned(3)

            tmp = s_sb[:, 0].rearrange("p h s -> p (h s)")
            for b in BR:
                for i in range(4):
                    half, t = i // 2, i % 2
                    name = f"p{b}_{i}"
                    full(dve, name)
                    gname = f"g{'ab'[half]}{b}_{t}"
                    wait_freed(dve, gname)
                    dst = tok[:, t, half * CB:(half + 1) * CB]
                    if b == BR[0]:
                        free(v.scalar_tensor_tensor(dst, gate[:, i, :], 1.0, bank(name), ALU.add, ALU.mult), name)
                    else:
                        tm = tmp[:, (i % 2) * CB:(i % 2 + 1) * CB]
                        free(v.scalar_tensor_tensor(tm, gate[:, i, :], 1.0, bank(name), ALU.add, ALU.mult), name)
                        settle()
                        ins = v.tensor_tensor(dst, dst, tm, ALU.add)
                        if b == BR[2]:
                            signal(ins, merged_ready, i + 1)
                        else:
                            do(ins)
            for i in (1, 3):
                full(dve, f"mT{i}")
                free(v.tensor_scalar(xT[:, 4 * (i % 2):4 * (i % 2) + 4, (i // 2) * P:(i // 2 + 1) * P],
                                     bank3(f"mT{i}", 4, P), 0.5, None, ALU.mult), f"mT{i}")
            dve.wait_ge(x_again, 32)
            for t in range(TT):
                for half in range(2):
                    name = f"wo{2 * t + half}"
                    full(dve, name)
                    dst = x1[:, t, half * CB:(half + 1) * CB]
                    free(v.tensor_tensor(dst, dst, bank(name), ALU.add), name)
                settle()
                signal(v.memset(small[:, 90:91], 0.0), x1_ready, t + 1)
                dve.wait_ge(x2_squares, t + 1)
                signal(v.tensor_scalar(small[:, 82 + t:83 + t], small[:, 80 + t:81 + t], 1.0 / D, EPS, ALU.mult,
                                       ALU.add), x2_mean, t + 1)
                dve.wait_ge(x2_root, t + 1)
                chain(v.reciprocal(small[:, 86 + t:87 + t], small[:, 84 + t:85 + t]))
                dst = tok[:, t, :].rearrange("p (k q) -> p q k", k=KD)
                signal(v.scalar_tensor_tensor(dst, x1[:, t, :].rearrange("p (q k) -> p q k", k=KD),
                                              small[:, 86 + t:87 + t], gain[:].rearrange("p (q k) -> p q k", k=KD),
                                              ALU.mult, ALU.mult), x2_normed, t + 1)
            for t in range(TT):
                name = f"x2T{2 * t + 1}"
                full(dve, name)
                free(v.tensor_copy(xT[:, 4:8, t * P:(t + 1) * P], bank3(name, 4, P)), name)
                full(dve, f"rl{t}")
                free(v.tensor_tensor(lg[:, t, :], bank(f"rl{t}")[:, 0:KR], rb[:], ALU.add), f"rl{t}")
            settle()

            def rtv(i, m=E):
                return rt[:, i, :, 0:m]

            def wide(ap, m):
                return bc(ap.unsqueeze(2), [P, TT, m])

            def first(values, top, m, key, dst):
                chain(v.tensor_tensor(rtv(key, m), values, wide(rs[:, top, :], m), ALU.is_equal))
                chain(v.tensor_tensor(rtv(key, m), rtv(key, m), bc(desc[:, 0:m].unsqueeze(1), [P, TT, m]), ALU.mult))
                chain(v.tensor_reduce(rs[:, 11, :], rtv(key, m), AX.X, ALU.max))
                chain(v.tensor_tensor(rtv(dst, m), rtv(key, m), wide(rs[:, 11, :], m), ALU.is_equal))

            gl, el = lg[:, :, 0:4], lg[:, :, 4:KR]
            chain(v.tensor_reduce(rs[:, 0, :], gl, AX.X, ALU.max))
            signal(v.tensor_tensor(rtv(0, 4), gl, wide(rs[:, 0, :], 4), ALU.subtract), g_shifted, 1)
            first(gl, 0, 4, 2, 3)
            dve.wait_ge(g_exped, 1)
            chain(v.tensor_reduce(rs[:, 1, :], rtv(1, 4), AX.X, ALU.add))
            do(v.reciprocal(rs[:, 2, :], rs[:, 1, :]))
            do(v.tensor_scalar(rtv(4, 4), rtv(3, 4), 1.0, -NEG, ALU.subtract, ALU.mult))
            settle()

            def by_group(ap):
                return ap.rearrange("p t (g e) -> p t g e", g=4)

            chain(v.tensor_tensor(by_group(rtv(5)), by_group(el), bc(rtv(3, 4).unsqueeze(3), [P, TT, 4, 8]), ALU.mult))
            chain(v.tensor_tensor(by_group(rtv(5)), by_group(rtv(5)), bc(rtv(4, 4).unsqueeze(3), [P, TT, 4, 8]), ALU.add))
            chain(v.tensor_reduce(rs[:, 5, :], rtv(5), AX.X, ALU.max))
            first(rtv(5), 5, E, 6, 7)
            chain(v.scalar_tensor_tensor(rtv(5), rtv(7), 2 * NEG, rtv(5), ALU.mult, ALU.add))
            chain(v.tensor_reduce(rs[:, 6, :], rtv(5), AX.X, ALU.max))
            signal(v.tensor_tensor(rs[:, 7, :], rs[:, 6, :], rs[:, 5, :], ALU.subtract), m_shifted, 1)
            first(rtv(5), 6, E, 6, 8)
            signal(v.tensor_tensor(rtv(9), rtv(7), rtv(8), ALU.add), picks_ready, 1)
            dve.wait_ge(m_exped, 1)
            chain(v.tensor_scalar(rs[:, 9, :], rs[:, 8, :], 1.0, None, ALU.add))
            chain(v.reciprocal(rs[:, 9, :], rs[:, 9, :]))
            chain(v.tensor_tensor(rs[:, 9, :], rs[:, 9, :], rs[:, 2, :], ALU.mult))
            chain(v.tensor_tensor(rs[:, 10, :], rs[:, 9, :], rs[:, 8, :], ALU.mult))
            do(v.tensor_tensor(rtv(7), rtv(7), wide(rs[:, 9, :], E), ALU.mult))
            do(v.tensor_tensor(rtv(8), rtv(8), wide(rs[:, 10, :], E), ALU.mult))
            settle()
            chain(v.tensor_tensor(rtv(10), rtv(7), rtv(8), ALU.add))
            full(dve, "pos")
            pp = bank("pos")[:, 0:TT * E].rearrange("p (t e) -> p t e", t=TT)
            do(v.tensor_reduce(small[:, 100:101], bank("pos")[:, TT * E:3 * E], AX.X, ALU.max))
            free(v.scalar_tensor_tensor(rtv(11), pp, 1.0, rtv(9), ALU.add, ALU.mult), "pos")
            settle()
            chain(v.tensor_scalar(rtv(11), rtv(11), -1.0, None, ALU.add))
            for t in range(TT):
                do(v.tensor_tensor(posx[:, t, 0:MAXR * E].rearrange("p (r e) -> p r e", r=MAXR),
                                   bc(rt[:, 11, t, :].unsqueeze(1), [P, MAXR, E]),
                                   bc(thr[:].unsqueeze(2), [P, MAXR, E]), ALU.subtract))
                do(v.tensor_copy(combx[:, t, 0:MAXR * E].rearrange("p (r e) -> p r e", r=MAXR),
                                 bc(rt[:, 10, t, :].unsqueeze(1), [P, MAXR, E])))
            do(v.memset(posx[:, :, MAXR * E:], -1.0))
            do(v.memset(combx[:, :, MAXR * E:], 0.0))
            do(v.tensor_scalar(small[0:1, 104:112], thr[0:1, :], small[0:1, 100:101], None, ALU.is_lt))
            settle()

            def one_hot(c, value):
                signal(v.tensor_tensor(hot[:], bc(iot[:].unsqueeze(1).unsqueeze(1), [P, TT, EG, SLOTS]),
                                       bc(posx[:, :, c].unsqueeze(3), [P, TT, EG, SLOTS]), ALU.is_equal),
                       hot_ready, value)

            def one_hot_weighted(c, value):
                settle()
                signal(v.tensor_tensor(hotw[:], hot[:], bc(combx[:, :, c].unsqueeze(3), [P, TT, EG, SLOTS]), ALU.mult),
                       hotw_ready, value)

            one_hot(slice(0, EG), 1)
            one_hot_weighted(slice(0, EG), 1)
            chain(v.tensor_reduce(small[0:1, 112:113], small[0:1, 104:112], AX.X, ALU.add))
            signal(v.tensor_copy(nrounds[:], small[0:1, 112:113]), rounds_ready, 1)
            dve.wait_ge(gather_done, 2)
            v.tensor_copy(xg[:, 4:8, :], xo[:, 1, :].rearrange("p (k s) -> p k s", k=4)).then_inc(xg_dve, 1)
            dve.wait_ge(rounds_ready, 1)
            nr = dve.value_load(nrounds[0:1, 0:1], min_val=1, max_val=MAXR)
            with dve.Fori(0, nr * NG) as it:
                dve.wait_ge(hotw_ready, it + 1)
                one_hot(bass.ds(it * EG + EG, EG), it + 2)
                dve.wait_ge(hotT_done, it + 1)
                v.tensor_copy(hotT[:], t_ps[:, 2 * P:4 * P].rearrange("p (t q) -> p t q", t=TT)).then_inc(hotT_copied, 1)
                dve.wait_ge(silu_done, it + 1)
                v.tensor_tensor(h[:], hs[:], h_ps[:, F:2 * F], ALU.mult).then_inc(h_ready, 1)
                dve.wait_ge(gather_done, it * 2 + 4)
                v.tensor_copy(xg[:, 4:8, :], xo[:, 1, :].rearrange("p (k s) -> p k s", k=4)).then_inc(xg_dve, 1)
                one_hot_weighted(bass.ds(it * EG + EG, EG), it + 2)
                dve.wait_ge(down_done, it * 2 + 2)
                v.tensor_copy(o_sb[:, CB:], xo[:, 1, :]).then_inc(o_dve, 1)
            for i in range(4):
                t, hf = i // 2, i % 2
                if i == 0:
                    dve.wait_ge(scatter_done, nr * (2 * NG))
                c = slice(hf * CB, (hf + 1) * CB)
                v.tensor_tensor(y_sb[:, t, c], y_ps[:, i, :], x1[:, t, c], ALU.add).then_inc(y_ready, 1)

        @block.tensor
        def _(pe):
            t_ = nc.tensor

            def open_(name):
                n = FI[name]
                if n >= 4:
                    pe.wait_ge(bank_free[n % 4], n // 4)

            def close(ins, name):
                ins.then_inc(bank_full, 1)

            def wait_freed(name):
                pe.wait_ge(bank_free[FI[name] % 4], FI[name] // 4 + 1)

            def loaded(name):
                pe.wait_ge(slot_full[LI[name] % RING], slot_count(name))

            def view(name, k, n):
                return slot(name)[:, 0:k * n].rearrange("p (k n) -> p k n", k=k)

            def by_tokens(name, w, t, c0, n, dst=None, k_n=KD, lhs=None):
                lhs = xT if lhs is None else lhs
                dst = bank(name)[:, 0:n] if dst is None else dst
                for k in range(k_n):
                    ins = t_.matmul(dst, lhs[:, k, t * P:(t + 1) * P], w[:, k, c0:c0 + n], start=k == 0, stop=k == k_n - 1)
                return ins

            def by_channels(w, cols, dst):
                for k in range(KD):
                    ins = t_.matmul(dst, w[:, k, cols], xT[:, k, :], start=k == 0, stop=k == KD - 1)
                return ins

            def channel_block(load, names):
                loaded(load)
                w = view(load, KD, CB)
                for i, name in enumerate(names):
                    open_(name)
                    for c in range(2):
                        ct = 2 * i + c
                        ins = by_channels(w, slice(ct * P, (ct + 1) * P), bank(name)[:, c * S:(c + 1) * S])
                    close(ins, name)

            pe.wait_ge(consts, 1)
            pe.wait_ge(rows_loaded, 16 * N_ROWDMA)
            open_("par")
            close(t_.transpose(bank("par")[:, 0:P], prow[:, :], ident[:, :]), "par")

            def turn_tokens(names, ready=None):
                for i, name in names:
                    t, k0 = i // 2, 4 * (i % 2)
                    if ready is not None:
                        ready(i)
                    open_(name)
                    for k in range(4):
                        ins = t_.transpose(bank(name)[:, k * P:(k + 1) * P], tok[:, t, (k0 + k) * P:(k0 + k + 1) * P],
                                           ident[:, :])
                    close(ins, name)

            turn_tokens([(i, f"xT{i}") for i in range(4)], lambda i: pe.wait_ge(x_normed, i // 2 + 1))
            for i in range(4):
                wait_freed(f"xT{i}")
            loaded("q")
            for t in range(TT):
                open_(f"q{t}")
                close(by_tokens(f"q{t}", view("q", KD, CB), t, 0, CB), f"q{t}")
            loaded("kva")
            kva = view("kva", KD, KVA)
            open_("kvs")
            for t in range(TT):
                ins = by_tokens("kvs", kva, t, 256, 256, bank("kvs")[:, t * 256:(t + 1) * 256])
            close(ins, "kvs")
            for i, name in enumerate(("kc", "vc")):
                open_(name)
                for g in range(GROUPS):
                    c0 = i * P + g * HD
                    for k in range(KD):
                        for j in range(2):
                            ins = t_.matmul(bank(name)[j * HD:(j + 1) * HD, g * S:(g + 1) * S], kva[:, k, c0:c0 + HD],
                                            xT[:, k, :], start=k == 0, stop=k == KD - 1)
                close(ins, name)
            loaded("kvb")
            for t in range(TT):
                open_(f"kvw{t}")
                close(by_tokens(f"kvw{t}", view("kvb", KD, KVB), t, 0, KVB), f"kvw{t}")
            channel_block("rx", ["rx0", "rx1"])
            pe.wait_ge(qk_normed, 1)
            for t in range(TT):
                open_(f"qT{t}")
                for c in range(CT):
                    ins = t_.transpose(bank(f"qT{t}")[:, c * P:(c + 1) * P], q_sb[:, t, c * P:(c + 1) * P], ident[:, :])
                close(ins, f"qT{t}")
            for br, name in enumerate(("kTs", "kTw")):
                open_(name)
                for g in range(GROUPS):
                    for t in range(TT):
                        ins = t_.transpose(bank(name)[:, g * S + t * P:g * S + (t + 1) * P], kd[:, br, t, g, :],
                                           ident[:, :])
                close(ins, name)
            loaded("cmp")
            pe.wait_ge(cx_ready, 1)
            open_("hid")
            w1 = slot("cmp")[:, :].rearrange("p (v l n) -> p v l n", v=2, l=LP)
            for kv in range(2):
                for lp in range(LP):
                    ins = t_.matmul(bank("hid")[:, kv * 32:kv * 32 + 30], w1[:, kv, lp, :], cx[:, kv, lp, :],
                                    start=lp == 0, stop=lp == LP - 1)
            close(ins, "hid")

            def scores(n):
                g, tt = UNITS[n]
                w = P * (tt + 1)
                for br in range(2):
                    if n:
                        pe.wait_ge(scores_maxed, 2 * n + br - 1)
                    for hh in range(HG):
                        hd = g * HG + hh
                        r = slice((hd % 2) * HD, (hd % 2 + 1) * HD)
                        ins = t_.matmul(s_ps[br][:, hh // 2, hh % 2, 0:w], qT[r, hd // 2, tt * P:(tt + 1) * P], kT[r, br, g, 0:w],
                                        start=True, stop=True)
                    ins.then_inc(scores_full, 1)

            channel_block("ry", ["ry0", "ry1"])
            wait_freed("kTw")
            wait_freed("hid")
            scores(0)
            pe.wait_ge(small_loaded, 16 * N_SMALLDMA)
            open_("cmp2")
            for kv in range(2):
                for g in range(GROUPS):
                    c0 = (kv * GROUPS + g) * HD
                    ins = t_.matmul(bank("cmp2")[0:NCMP, c0:c0 + HD], hid[:, kv, g * NCMP:(g + 1) * NCMP], w2[:, kv, :],
                                    start=True, stop=True)
            close(ins, "cmp2")
            pe.wait_ge(u_ready, 1)
            for i, gname in enumerate("ri"):
                for hf in range(2):
                    name = f"{gname}{hf}"
                    open_(name)
                    for c in range(2):
                        ct = 2 * hf + c
                        ins = t_.matmul(bank(name)[:, c * S:(c + 1) * S], wbd[:, i, ct, :], u[:, ct, :],
                                        start=True, stop=True)
                    close(ins, name)
            pe.wait_ge(kc_normed, 1)
            open_("kcT")
            for g in range(GROUPS):
                ins = t_.transpose(bank("kcT")[:, g * 16:g * 16 + NCMP], kcd[0:NCMP, g, :], ident[0:NCMP, 0:NCMP])
            close(ins, "kcT")
            channel_block("sb", ["sb0", "sb1"])
            wait_freed("kcT")
            for a in range(2):
                open_(f"Sc{a}")
                for tt in range(TT):
                    for hp in range(HEADS // 2):
                        r = slice(a * HD, (a + 1) * HD)
                        c0 = (tt * HEADS // 2 + hp) * 16
                        ins = t_.matmul(bank(f"Sc{a}")[:, c0:c0 + NCMP], qT[r, hp, tt * P:(tt + 1) * P],
                                        cmpT[r, 2 * hp // HG, 0:NCMP], start=True, stop=True)
                close(ins, f"Sc{a}")

            def attend(n):
                g, tt = UNITS[n]
                for br in range(2):
                    pe.wait_ge(probs_ready, 2 * n + br + 1)
                    for sbk in range(tt + 1):
                        name = f"pt{n}_{br}{sbk}"
                        open_(name)
                        for hh in range(HG):
                            ins = t_.transpose(bank(name)[:, hh * P:(hh + 1) * P],
                                               s_sb[:, br, hh, sbk * P:(sbk + 1) * P], ident[:, :])
                        close(ins, name)
                if n == 0:
                    pe.wait_ge(pc_ready, 1)
                name = f"ptc{n}"
                open_(name)
                close(t_.transpose(bank(name)[:, 0:P], pc[:, tt, g * HG:(g + 1) * HG, :].rearrange("p h n -> p (h n)"),
                                   ident[:, :]), name)
                name = f"o{n}"
                open_(name)
                for src in fills_of_unit(n)[:-1]:
                    wait_freed(src)
                for hh in range(HG):
                    dst = bank(name)[(hh % 2) * HD:(hh % 2 + 1) * HD, (hh // 2) * P:(hh // 2 + 1) * P]
                    first = True
                    for br, vv in ((0, kvs), (1, kvw)):
                        for sbk in range(tt + 1):
                            t_.matmul(dst, vv[:, sbk, P + g * HD:P + (g + 1) * HD], pT[:, br, sbk, hh, :],
                                      start=first, stop=False)
                            first = False
                    ins = t_.matmul(dst, vbd[:, g, hh, :], pTc[:], start=False, stop=True)
                close(ins, name)

            channel_block("sc", ["sc0", "sc1"])
            attend(0)
            scores(1)
            channel_block("sh", ["sh0", "sh1"])
            attend(1)
            scores(2)

            def gates(b, half):
                name = f"g{'ab'[half]}{b}"
                loaded(name)
                for t in range(TT):
                    open_(f"{name}_{t}")
                    close(by_tokens(f"{name}_{t}", view(name, KD, CB), t, 0, CB), f"{name}_{t}")

            def product(b):
                loaded(f"w{b}")
                for i in range(4):
                    half, t = i // 2, i % 2
                    name = f"p{b}_{i}"
                    open_(name)
                    close(by_tokens(name, view(f"w{b}", CT, D), t, half * CB, CB, k_n=CT, lhs=yT[:, b]), name)

            gates(0, 0)
            attend(2)
            scores(3)
            gates(0, 1)
            attend(3)
            pe.wait_ge(y_rnn_ready, 1)
            product(0)
            gates(2, 0)
            gates(2, 1)
            pe.wait_ge(y_sc_ready, 1)
            product(2)
            gates(1, 0)
            gates(1, 1)
            for n in range(4):
                wait_freed(f"o{n}")
            product(1)
            pe.wait_ge(merged_ready, 4)
            turn_tokens([(i, f"mT{i}") for i in range(4)])
            loaded("wo0")
            loaded("wo1")
            for t in range(TT):
                wait_freed(f"mT{2 * t}")
                wait_freed(f"mT{2 * t + 1}")
                for half in range(2):
                    name = f"wo{2 * t + half}"
                    open_(name)
                    close(by_tokens(name, view(f"wo{half}", KD, CB), t, 0, CB), name)
            for t in range(TT):
                pe.wait_ge(x2_normed, t + 1)
                turn_tokens([(i, f"x2T{i}") for i in (2 * t, 2 * t + 1)])
                wait_freed(f"x2T{2 * t}")
                wait_freed(f"x2T{2 * t + 1}")
                open_(f"rl{t}")
                close(by_tokens(f"rl{t}", rw, t, 0, KR), f"rl{t}")
            pe.wait_ge(picks_ready, 1)
            open_("pos")
            A = rt[:, 9]
            t_.matmul(bank("pos")[:, 0:E], tri[:, :], A[:, 0, :], start=True, stop=True)
            t_.matmul(bank("pos")[:, E:2 * E], tri[:, :], A[:, 1, :], start=True, stop=False)
            t_.matmul(bank("pos")[:, E:2 * E], ones[:, :], A[:, 0, :], start=False, stop=True)
            t_.matmul(bank("pos")[:, 2 * E:3 * E], ones[:, :], A[:, 0, :], start=True, stop=False)
            close(t_.matmul(bank("pos")[:, 2 * E:3 * E], ones[:, :], A[:, 1, :], start=False, stop=True), "pos")

            def gather(value):
                pe.wait_ge(hot_ready, value)
                hv = hot[:].rearrange("p t e s -> p t (e s)")
                for b in range(2):
                    for k in range(4):
                        for t in range(TT):
                            ins = t_.matmul(xo[:, b, k * P:(k + 1) * P], tok[:, t, (4 * b + k) * P:(4 * b + k + 1) * P],
                                            hv[:, t, :], start=t == 0, stop=t == TT - 1)
                    ins.then_inc(gather_done, 1)

            for n in ("x2T3", "rl1", "x2T2", "pos"):
                wait_freed(n)
            for i in range(4):
                t_.matmul(y_ps[:, i, :], nmask[0:1, 1, 0:1].to_broadcast([1, P]), cmask[0:1, 0:1].to_broadcast([1, CB]),
                          start=True, stop=True)
            gather(1)
            pe.wait_ge(rounds_ready, 1)
            nr = pe.value_load(nrounds[0:1, 0:1], min_val=1, max_val=MAXR)
            with pe.Fori(0, nr * NG) as it:
                pe.wait_ge(xg_act, it + 1)
                pe.wait_ge(xg_dve, it + 1)
                for j in range(4):
                    s = MS[j]
                    pe.wait_ge(slot_full[s], it * 32 + (MBASE[j] + 32))
                    w = ring[:, s, :].rearrange("p (m e k f) -> p e k m f", m=2, e=EG, k=2)
                    for k in range(2):
                        for e in range(EG):
                            ins = t_.matmul(h_ps[e * SLOTS:(e + 1) * SLOTS, :].rearrange("p (m f) -> p m f", m=2),
                                            xg[:, 2 * j + k, e * SLOTS:(e + 1) * SLOTS], w[:, e, k],
                                            start=(j == 0 and k == 0), stop=(j == 3 and k == 1),
                                            skip_group_check=True)
                    ins.then_inc(kpair_done, 1)
                pe.wait_ge(hotw_ready, it + 1)
                for t in range(TT):
                    ins = t_.transpose(t_ps[:, (2 + t) * P:(3 + t) * P], hotw[:, t].rearrange("p e s -> p (e s)"),
                                       ident[:, :])
                ins.then_inc(hotT_done, 1)
                gather(it + 2)
                pe.wait_ge(h_ready, it + 1)
                for c in range(2):
                    ins = t_.transpose(t_ps[:, c * P:(c + 1) * P], h[:].rearrange("p (q c) -> p c q", c=2)[:, c, :],
                                       ident[:, :])
                ins.then_inc(hT_done, 1)
                pe.wait_ge(hT_copied, it + 1)
                for hf in range(2):
                    s = MS[4 + hf]
                    pe.wait_ge(slot_full[s], it * 32 + (MBASE[4 + hf] + 32))
                    pe.wait_ge((xg_act, xg_dve)[hf], it + 2)
                    w = ring[:, s, :].rearrange("p (e c n) -> p e c n", e=EG, c=2)
                    for c in range(2):
                        for e in range(EG):
                            ins = t_.matmul(xo[e * SLOTS:(e + 1) * SLOTS, hf, :], hT[:, c, e * SLOTS:(e + 1) * SLOTS],
                                            w[:, e, c, :], start=c == 0, stop=c == 1, skip_group_check=True)
                    ins.then_inc(down_done, 1)
                pe.wait_ge(hotT_copied, it + 1)
                for hf in range(2):
                    pe.wait_ge((o_act, o_dve)[hf], it + 1)
                    for t in range(TT):
                        ins = t_.matmul(y_ps[:, 2 * t + hf, :], hotT[:, t, :], o_sb[:, hf * CB:(hf + 1) * CB],
                                        start=False, stop=False, skip_group_check=True)
                    ins.then_inc(scatter_done, 1)


NAMES = ['x', 'mix_norm', 'w_in', 'rnn_conv_w', 'rnn_conv_b', 'rg_wa', 'rg_ba', 'rg_wx', 'rg_bx', 'rg_lambda',
         'cmp_pe', 'cmp_w1', 'cmp_b1', 'cmp_w2', 'cmp_b2', 'q_norm', 'k_norm', 'sc_conv_w',
         'w_rnn_out', 'w_nsa_out', 'w_sc_out', 'w_out', 'ffn_norm',
         'router_group_w', 'router_group_b', 'router_expert_w', 'router_expert_b',
         'exp_w_gate', 'exp_w_up', 'exp_w_down']


def kernel(**inputs):
    import concourse.bacc as bacc
    from concourse.bass_utils import run_bass_kernel_spmd

    nc = bacc.Bacc("TRN2", target_bir_lowering=False, num_devices=1)
    arrays, args = {}, []
    for name in NAMES:
        a = np.ascontiguousarray(inputs[name])
        arrays[f"in_{name}"] = a
        args.append(nc.dram_tensor(f"in_{name}", a.shape, mybir.dt.from_np(a.dtype), kind="ExternalInput").ap())
    args.append(nc.dram_tensor("out_0", (1, S, D), fp32, kind="ExternalOutput").ap())
    trunk(nc, *args)
    r = run_bass_kernel_spmd(nc, [arrays], core_ids=[0])
    return r.results[0]["out_0"]
```

```python
from contextlib import ExitStack

import numpy as np

import concourse.bass as bass
from concourse import mybir

fp32 = mybir.dt.float32
f32r = mybir.dt.float32r
i32 = mybir.dt.int32
ALU = mybir.AluOpType
ACT = mybir.ActivationFunctionType
AX = mybir.AxisListType

P = 128
S, D = 256, 1024
TT = S // P
KD = D // P
W4 = 512
CT = W4 // P
HD = 64
HEADS, GROUPS = 8, 2
HG = HEADS // GROUPS
NCMP, CL, CS = 15, 32, 16
LP = CL // 2
RNN_TAPS, SC_TAPS = 4, 3
NEG = -1e30
EPS = 1e-6
E, EG = 32, 4
NG = E // EG
F = 256
SLOTS = 32
MAXR = S // SLOTS
RING = 3
NLOAD = 6
NDOUBLE = 3
SLOT = 4096
CB = 512

C_RX, C_RY, C_Q, C_KC, C_KSL, C_KWN, C_SB, C_SC, C_SH, C_MG = (
    0, 512, 1024, 1536, 1792, 2048, 2328, 2840, 3352, 3864)
KVA = C_KWN - C_KC
KVB = C_SB - C_KWN
BR = (0, 2, 1)

LOADS = (["q", "kva", "kvb", "rx", "cmp", "ry", "sb", "sc", "sh"]
         + [f"{x}{b}" for b in BR for x in ("ga", "gb", "w")] + ["wo0", "wo1"])
LI = {n: i for i, n in enumerate(LOADS)}
UNITS = [(0, 0), (1, 0), (0, 1), (1, 1)]


def fills_of_unit(u):
    tt = UNITS[u][1]
    return [f"pt{u}_{br}{sb}" for br in range(2) for sb in range(tt + 1)] + [f"ptc{u}", f"o{u}"]


FILLS = ([f"xT{i}" for i in range(4)] + ["q0", "q1", "kva0", "kva1", "kvb0", "kvb1", "kc", "vc", "par", "rx0", "rx1",
         "hid", "qT0", "qT1", "kTs", "kTw", "ry0", "ry1", "cmp2", "r0", "r1", "i0", "i1", "sb0", "sb1", "kcT",
         "sc0", "sc1", "Sc0", "Sc1", "sh0", "sh1"] + fills_of_unit(0) + ["ga0_0", "ga0_1"] + fills_of_unit(1)
         + ["gb0_0", "gb0_1"] + [f"p0_{i}" for i in range(4)] + fills_of_unit(2)
         + ["ga2_0", "ga2_1", "gb2_0", "gb2_1"] + fills_of_unit(3) + [f"p2_{i}" for i in range(4)]
         + ["ga1_0", "ga1_1", "gb1_0", "gb1_1"] + [f"p1_{i}" for i in range(4)]
         + [f"mT{i}" for i in range(4)] + [f"wo{i}" for i in range(4)]
         + ["x2T0", "x2T1", "x2T2", "x2T3", "rl0", "rl1", "pos"])
FI = {n: i for i, n in enumerate(FILLS)}
SPLIT = [n for n in LOADS if n != "cmp"]
SI = {n: 2 * i for i, n in enumerate(SPLIT)}
KH = KD // 2
WB = [f"w{b}" for b in BR]
MADE = {n: (f"{n}_0", f"{n}_1") if n[0] == "g" else (f"{n}0", f"{n}1") for n in SPLIT if n not in WB}
MADE.update(wo0=("wo0", "wo1"), wo1=("wo2", "wo3"))
ENDED = [(f"p{n[1]}_{2 * hf + 1}" if n in WB else MADE[n][1] if hf else None) for n in SPLIT for hf in range(2)]

ROWS, _at = {}, 0
for _n, _k in (("cw", 16), ("cb", 4), ("sw", 12), ("ba", 4), ("bx", 4), ("lam", 4), ("b1", 2), ("qn", 1),
               ("kn", 3), ("pe", 32)):
    ROWS[_n] = _at
    _at += _k
NROWS = _at
KR = 36


def trunk(nc, x, mix_norm, w_in, rnn_conv_w, rnn_conv_b, rg_wa, rg_ba, rg_wx, rg_bx, rg_lambda,
          cmp_pe, cmp_w1, cmp_b1, cmp_w2, cmp_b2, q_norm, k_norm, sc_conv_w,
          w_rnn_out, w_nsa_out, w_sc_out, w_out, ffn_norm,
          router_group_w, router_group_b, router_expert_w, router_expert_b,
          exp_w_gate, exp_w_up, exp_w_down, out):
    ctx = ExitStack()
    with ctx:
        def sb(name, shape, dt=fp32):
            return ctx.enter_context(nc.sbuf_tensor(name, shape, dt))

        def sem(name):
            return ctx.enter_context(nc.semaphore(name))

        ring = sb("ring", [P, RING, SLOT])
        def sb_split(name, shape):
            return split.enter_context(nc.sbuf_tensor(name, shape, f32r))

        split = ExitStack()
        with split:
            xh = sb_split("xh", [P, KD, S])
            xl = sb_split("xl", [P, KD, S])
            wh = sb_split("wh", [P, 2, KH * CB])
            wl = sb_split("wl", [P, 2, KH * CB])
        odd = [sb(f"odd{i}", [P, SLOT]) for i in range(NDOUBLE)]
        tok = sb("tok", [P, TT, D])
        yT = sb("yT", [P, 3, CT, S])
        gate = sb("gate", [P, 4, CB])
        pcol = sb("pcol", [P, NROWS])
        ident = sb("ident", [P, P])
        tri = sb("tri", [P, P])
        ones = sb("ones", [P, P])
        cmask = sb("cmask", [P, 2 * P])
        nmask = sb("nmask", [P, TT, NCMP])
        ngany = sb("ngany", [P, TT])
        iot = sb("iot", [P, SLOTS])
        desc = sb("desc", [P, E])
        thr = sb("thr", [P, MAXR])
        wbd = sb("wbd", [P, 2, CT, P])
        w2 = sb("w2", [P, 2, HD])
        b2 = sb("b2", [NCMP, 2, HD])
        rw = sb("rw", [P, KD, KR])
        rb = sb("rb", [P, KR])
        small = sb("small", [P, P])
        nrounds = sb("nrounds", [1, 1], i32)
        split = ExitStack()
        with split:
            yh, yl = sb_split("yh", [P, CT, S]), sb_split("yl", [P, CT, S])
        a_rnn = sb("a_rnn", [P, 5 * CT * S + 16])
        a_sc = sb("a_sc", [P, 2 * CT * S + 16])
        a_att = sb("a_att", [P, 9216 + 320])
        a_moe = sb("a_moe", [P, 1536])

        def part(area, at, shape):
            n = int(np.prod(shape))
            v = area[:, at:at + n]
            names = "abcd"[:len(shape)]
            return v.rearrange(f"p ({' '.join(names)}) -> p {' '.join(names)}", **dict(zip(names, shape)))

        CTS = CT * S
        kdup = part(a_att, 6144, (TT, 2 * GROUPS, 2, HD))
        rxp = part(a_rnn, 0, (CT, S + 4))
        u = part(a_rnn, CTS + 16, (CT, S))
        rg = part(a_rnn, 2 * CTS + 16, (CT, S))
        ig = part(a_rnn, 3 * CTS + 16, (CT, S))
        rr = part(a_rnn, 4 * CTS + 16, (CT, S))
        root = part(a_rnn, 0, (CT, S))
        zp = part(a_sc, 0, (CT, S + 4))
        scc = part(a_sc, CTS + 16, (CT, S))
        q_sb = part(a_att, 0, (TT, W4))
        kvs = part(a_att, 1024, (TT, 256))
        kvw = part(a_att, 1536, (TT, 256))
        qT = part(a_att, 2048, (CT, S))
        kT = part(a_att, 3072, (2, GROUPS, S))
        s_sb = part(a_att, 4096, (2, HG, S))
        pT = part(a_att, 6144, (2, TT, HG, P))
        pTc = part(a_att, 8192, (P,))
        pc = part(a_att, 8320, (TT, HEADS, 32))
        cmpT = part(a_att, 8832, (GROUPS, 16))
        kcd = part(a_att, 8864, (GROUPS, P))
        ngs = part(a_att, 9120, (TT, 24))
        coef = part(a_att, 9168, (4, 16))
        l_sb = part(a_att, 9232, (2, HG))
        nm = part(a_att, 9240, (2, HG))
        ssq = part(a_att, 9248, (TT, 12))
        sq12 = part(a_att, 9280, (TT, 12))
        prow = part(a_att, 8192, (P,))
        kcv = part(a_att, 4096, (2, GROUPS, S))
        sqs = part(a_att, 5120, (TT, W4))
        kd = part(a_att, 5120, (2, TT, GROUPS, P))
        cx = part(a_att, 6144, (2, LP, GROUPS * NCMP))
        hid = part(a_att, 7104, (2, GROUPS * NCMP))
        kc_sb = part(a_att, 7168, (GROUPS, HD))
        kc_sq = part(a_att, 7296, (GROUPS, HD))
        vbd = part(a_moe, 1024, (GROUPS, HG, HD))
        gain = yT[:, 0].rearrange("p c s -> p (c s)")
        even = [part(a_att, 0, (SLOT,)), part(a_att, SLOT, (SLOT,)), part(a_rnn, 0, (SLOT,)),
                ring[:, 2, :], ring[:, 0, :], ring[:, 1, :]]
        x1 = part(a_sc, 0, (TT, D))
        x2T = gate[:].rearrange("p a n -> p (a n)").rearrange("p (k s) -> p k s", k=KD)
        xg = yT[:, 1].rearrange("p c s -> p (c s)").rearrange("p (k s) -> p k s", k=KD)
        o_sb = yT[:, 2].rearrange("p c s -> p (c s)")
        posx = part(a_att, 2 * SLOT, (TT, MAXR * E + EG))
        combx = part(a_att, 2 * SLOT + 640, (TT, MAXR * E + EG))
        hot = part(a_moe, 0, (TT, EG, SLOTS))
        hotw = part(a_moe, 256, (TT, EG, SLOTS))
        hotT = part(a_moe, 512, (TT, P))
        hs = part(a_moe, 768, (F,))
        h = part(a_moe, 1024, (F,))
        hT = part(a_moe, 1280, (2, P))
        lg = part(a_rnn, SLOT, (TT, KR))
        rt = part(a_rnn, SLOT + 80, (12, TT, E))
        rs = part(a_rnn, SLOT + 860, (12, TT))

        psum = ctx.enter_context(nc.psum_tensor("psum", [P, 8, 512], fp32))

        def bank(n):
            return psum[:, FI[n] % 4, :]

        def bank3(n, a, b):
            return bank(n)[:, 0:a * b].rearrange("p (a b) -> p a b", a=a)

        s_ps = [psum[:, b:b + 2, :].rearrange("p a (h s) -> p h a s", h=2) for b in (4, 6)]
        y_ps = psum[:, 0:4, :]
        xo = psum[:, 4:6, :]
        h_ps = psum[:, 6, :]
        t_ps = psum[:, 7, :]

        slot_full = [sem(f"slot_full{i}") for i in range(RING)]
        even_full = [sem(f"even_full{i}") for i in range(NLOAD)]
        odd_full = [sem(f"odd_full{i}") for i in range(NDOUBLE)]
        hi_ready, lo_ready, hi_used, lo_used, xh_ready = map(sem, (
            "hi_ready", "lo_ready", "hi_used", "lo_used", "xh_ready"))
        bank_full = sem("bank_full")
        bank_free = [sem(f"bank_free{i}") for i in range(4)]
        x_loaded = [sem(f"x_loaded{t}") for t in range(TT)]
        gain_loaded, rows_loaded, small_loaded, x_again = map(sem, (
            "gain_loaded", "rows_loaded", "small_loaded", "x_again"))
        ident_ready, consts, pads = sem("ident_ready"), sem("consts"), sem("pads")
        dve_chain, act_chain, pool_chain = sem("dve_chain"), sem("act_chain"), sem("pool_chain")
        x_squares, x_mean, x_root, x_normed = map(sem, ("x_squares", "x_mean", "x_root", "x_normed"))
        qk_mean, qk_root, qk_normed = map(sem, ("qk_mean", "qk_root", "qk_normed"))
        lam_ready, lam_exp, lru_scale = map(sem, ("lam_ready", "lam_exp", "lru_scale"))
        u_ready, r_tanh, th_ready, negth_ready, root_ready = map(sem, (
            "u_ready", "r_tanh", "th_ready", "negth_ready", "root_ready"))
        cx_ready, kc_mean, kc_root, kc_normed = map(sem, ("cx_ready", "kc_mean", "kc_root", "kc_normed"))
        sc_shifted, sc_exped, pc_ready = map(sem, ("sc_shifted", "sc_exped", "pc_ready"))
        scores_full, scores_maxed, scores_exped, probs_ready = map(sem, (
            "scores_full", "scores_maxed", "scores_exped", "probs_ready"))
        y_rnn_ready, y_sc_ready, merged_ready = map(sem, ("y_rnn_ready", "y_sc_ready", "merged_ready"))
        yh_ready, yl_ready = map(sem, ("yh_ready", "yl_ready"))
        x2_squares, x2_mean, x2_root, x2_normed = map(sem, (
            "x2_squares", "x2_mean", "x2_root", "x2_normed"))
        g_shifted, g_exped, m_shifted, m_exped, picks_ready, rounds_ready = map(sem, (
            "g_shifted", "g_exped", "m_shifted", "m_exped", "picks_ready", "rounds_ready"))
        kpair_done, down_done, gather_done, hotT_done, hT_done, scatter_done = map(sem, (
            "kpair_done", "down_done", "gather_done", "hotT_done", "hT_done", "scatter_done"))
        hot_ready, hotw_ready, silu_done, h_ready, hT_copied, hotT_copied = map(sem, (
            "hot_ready", "hotw_ready", "silu_done", "h_ready", "hT_copied", "hotT_copied"))
        xg_act, xg_dve, o_act, o_dve, y_ready, stored = map(sem, (
            "xg_act", "xg_dve", "o_act", "o_dve", "y_ready", "stored"))

        def copies(name):
            return 2 if name in ("cmp",) else 1

        def slot_count(name):
            i = LI[name]
            return 16 * sum(copies(LOADS[j]) for j in range(i % RING, i + 1, RING))


        def place(j, odd_group):
            return (odd[j][:, :], odd_full[j]) if odd_group and j < NDOUBLE else (even[j], even_full[j])

        def loaded(eng, name):
            eng.wait_ge(slot_full[LI[name] % RING], slot_count(name))

        def slot(name):
            return ring[:, LI[name] % RING, :]

        def full(eng, name):
            eng.wait_ge(bank_full, FI[name] + 1)

        def freed(ins, name):
            ins.then_inc(bank_free[FI[name] % 4], 1)

        def used(eng, name):
            if name in SI:
                eng.wait_ge(lo_ready, SI[name] + 2)
            else:
                full(eng, "hid")

        def high_free(eng, n):
            if n >= 2:
                eng.wait_ge(hi_used, n - 1)
                eng.wait_ge(lo_ready, n - 1)

        def low_free(eng, n):
            if n >= 2:
                if ENDED[n - 2]:
                    full(eng, ENDED[n - 2])
                else:
                    eng.wait_ge(lo_used, ENDED[:n - 1].count(None))

        def halves(n, parts):
            name, hf = SPLIT[n // 2], n % 2
            if name in WB:
                src = slot(name).rearrange("p (k n) -> p k n", k=CT)[:, :, hf * CB:(hf + 1) * CB]
                return src, parts[:, n % 2, :].rearrange("p (k n) -> p k n", k=CT)
            w = {"kvb": KVB}.get(name, CB)
            src = slot(name)[:, hf * KH * w:(hf + 1) * KH * w].rearrange("p (k n) -> p k n", k=KH)
            return src, parts[:, n % 2, 0:KH * w].rearrange("p (k n) -> p k n", k=KH)

        def bc(ap, shape):
            return ap.to_broadcast(shape)

        block = ctx.enter_context(nc.Block())

        wg_v = exp_w_gate[0].rearrange("(g e) (p k) f -> g p e (k f)", e=EG, p=P)
        wu_v = exp_w_up[0].rearrange("(g e) (p k) f -> g p e (k f)", e=EG, p=P)
        wd_v = exp_w_down[0].rearrange("(g e) (p c) n -> g p e c n", e=EG, p=P)
        win_v = w_in[0].rearrange("(k p) n -> p k n", p=P)

        @block.sync
        def _(sp):
            def columns(name, c0, n):
                dst = slot(name)[:, 0:KD * n].rearrange("p (k n) -> p k n", k=KD)
                sp.dma_start(dst, win_v[:, :, c0:c0 + n]).then_inc(slot_full[LI[name] % RING], 16)

            def whole(name, w):
                dst = slot(name)[:, :].rearrange("p (k n) -> p k n", k=CT)
                sp.dma_start(dst, w[0].rearrange("(k p) n -> p k n", p=P)).then_inc(slot_full[LI[name] % RING], 16)

            def experts(g, j, odd_group=False):
                dst, is_full = place(j, odd_group)
                if j < 4:
                    dst = dst.rearrange("p (m e n) -> p m e n", m=2, e=EG)
                    for m, w in enumerate((wg_v, wu_v)):
                        src = w[g][:, :, j * 2 * F:(j + 1) * 2 * F] if isinstance(g, int) else \
                            w[bass.ds(g, 1), :, :, j * 2 * F:(j + 1) * 2 * F].rearrange("g p e n -> p (g e) n")
                        sp.dma_start(dst[:, m], src).then_inc(is_full, 16)
                else:
                    dst = dst.rearrange("p (e c n) -> p e c n", e=EG, c=2)
                    for c in range(2):
                        lo = (j - 4) * CB
                        src = wd_v[g][:, :, c, lo:lo + CB] if isinstance(g, int) else \
                            wd_v[bass.ds(g, 1), :, :, c, lo:lo + CB].rearrange("g p e n -> p (g e) n")
                        sp.dma_start(dst[:, :, c, :], src).then_inc(is_full, 16)

            for t in range(TT):
                sp.dma_start(tok[:, t, :], x[0, t * P:(t + 1) * P, :]).then_inc(x_loaded[t], 16)
            for i, name in enumerate(LOADS):
                if name == "w1":
                    full(sp, "o3")
                    experts(0, 0)
                    experts(0, 1)
                if i >= RING:
                    used(sp, LOADS[i - RING])
                if name == "q":
                    columns(name, C_Q, CB)
                elif name == "kva":
                    columns(name, C_KC, KVA)
                elif name == "kvb":
                    columns(name, C_KWN, KVB)
                elif name == "cmp":
                    for kv in range(2):
                        dst = slot(name)[:, kv * LP * P:(kv + 1) * LP * P].rearrange("p (l n) -> p l n", l=LP)
                        sp.dma_start(dst, cmp_w1[0, kv].rearrange("(l p) n -> p l n", p=P)
                                     ).then_inc(slot_full[i % RING], 16)
                elif name in ("rx", "ry", "sb", "sc", "sh"):
                    columns(name, dict(rx=C_RX, ry=C_RY, sb=C_SB, sc=C_SC, sh=C_SH)[name], CB)
                elif name[0] == "g":
                    columns(name, C_MG + int(name[2]) * D + (name[1] == "b") * CB, CB)
                elif name[0:2] == "wo":
                    dst = slot(name)[:, :].rearrange("p (k n) -> p k n", k=KD)
                    sp.dma_start(dst, w_out[0].rearrange("(k p) n -> p k n", p=P)[:, :, int(name[2]) * CB:][:, :, 0:CB]
                                 ).then_inc(slot_full[i % RING], 16)
                else:
                    whole(name, (w_rnn_out, w_nsa_out, w_sc_out)[int(name[1])])

            used(sp, "w1")
            experts(0, 3)
            full(sp, "p1_3")
            experts(0, 2)
            for j, name in ((4, "wo0"), (5, "wo1")):
                used(sp, name)
                experts(0, j)

            full(sp, "wo3")
            for j in range(NDOUBLE):
                experts(1, j, True)

            def reload(g, it, odd_group, js):
                for j in js:
                    if j < NDOUBLE:
                        sp.wait_ge(kpair_done, it * 4 + (j - 7))
                    elif j < 4:
                        sp.wait_ge(kpair_done, it * 4 + (j - 3))
                    else:
                        sp.wait_ge(down_done, it * 2 + (j - 5))
                    experts(g, j, odd_group)

            reload(1, 1, True, range(NDOUBLE, NLOAD))
            with sp.Fori(1, NG // 2) as i:
                for b in range(2):
                    reload(i * 2 + b, i * 2 + b, b == 1, range(NLOAD))
            sp.wait_ge(rounds_ready, 1)
            nr = sp.value_load(nrounds[0:1, 0:1], min_val=1, max_val=MAXR)
            with sp.If(nr > 1):
                with sp.Fori(1, nr) as r:
                    with sp.Fori(0, NG // 2) as i:
                        for b in range(2):
                            reload(i * 2 + b, r * NG + i * 2 + b, b == 1, range(NLOAD))
            sp.end_ifs()
            for i in range(4):
                sp.wait_ge(y_ready, i + 1)
                t, hf = i // 2, i % 2
                sp.dma_start(out[0, t * P:(t + 1) * P, hf * CB:(hf + 1) * CB], x1[:, t, hf * CB:(hf + 1) * CB]
                             ).then_inc(stored, 16)
            sp.wait_ge(stored, 64)

        @block.gpsimd
        def _(pool):
            g = nc.gpsimd
            n = [0]

            def step(ins):
                n[0] += 1
                ins.then_inc(pool_chain, 1)

            def settle():
                pool.wait_ge(pool_chain, n[0])

            step(g.memset(ident[:], 0.0))
            settle()
            g.affine_select(out=ident[:], in_=ident[:], compare_op=ALU.not_equal, fill=1.0, base=0,
                            pattern=[[-1, P]], channel_multiplier=1).then_inc(ident_ready, 1)
            step(g.memset(prow[:], 0.0))
            step(g.memset(tri[:], 1.0))
            step(g.memset(cmask[:], 0.0))
            step(g.memset(nmask[:], 0.0))
            step(g.memset(ngany[:], 1.0))
            settle()
            def rows(name, src, c0=0, c1=P):
                r = ROWS[name]
                g.dma_start(prow[r:r + src.shape[0], c0:c1], src).then_inc(rows_loaded, 16)
            rows("cw", rnn_conv_w[0].rearrange("a (c p) -> (a c) p", p=P))
            rows("cb", rnn_conv_b.rearrange("a (c p) -> (a c) p", p=P))
            rows("sw", sc_conv_w[0].rearrange("a (c p) -> (a c) p", p=P))
            rows("ba", rg_ba[0].rearrange("(c h) i -> c (h i)", h=2))
            rows("bx", rg_bx[0].rearrange("(c h) i -> c (h i)", h=2))
            rows("lam", rg_lambda.rearrange("a (c p) -> (a c) p", p=P))
            rows("b1", cmp_b1[0])
            for c in (0, HD):
                rows("qn", q_norm, c, c + HD)
                rows("kn", k_norm[0], c, c + HD)
            rows("pe", cmp_pe[0].rearrange("v (l j) d -> (v l) (j d)", j=2))
            step(g.affine_select(out=cmask[:, P:], in_=cmask[:, P:], compare_op=ALU.is_ge, fill=NEG, base=0,
                                 pattern=[[-1, P]], channel_multiplier=1))
            step(g.affine_select(out=nmask[:], in_=nmask[:], compare_op=ALU.is_ge, fill=NEG, base=1 - CL,
                                 pattern=[[P, TT], [-CS, NCMP]], channel_multiplier=1))
            step(g.affine_select(out=ngany[:], in_=ngany[:], compare_op=ALU.is_ge, fill=0.0, base=1 - CL,
                                 pattern=[[P, TT]], channel_multiplier=1))
            step(g.affine_select(out=tri[:], in_=tri[:], compare_op=ALU.is_gt, fill=0.0, base=0,
                                 pattern=[[1, P]], channel_multiplier=-1))
            step(g.memset(ones[:], 1.0))
            step(g.iota(iot[:], pattern=[[1, SLOTS]], base=0, channel_multiplier=0, allow_small_or_imprecise_dtypes=True))
            step(g.iota(desc[:], pattern=[[-1, E]], base=E, channel_multiplier=0, allow_small_or_imprecise_dtypes=True))
            step(g.iota(thr[:], pattern=[[SLOTS, MAXR]], base=0, channel_multiplier=0, allow_small_or_imprecise_dtypes=True))
            settle()
            g.memset(rxp[:, :, 0:3], 0.0).then_inc(consts, 1)
            step(g.memset(wbd[:], 0.0))
            settle()
            for i, w in enumerate((rg_wa, rg_wx)):
                for hh in range(2):
                    g.dma_start(wbd[hh * HD:(hh + 1) * HD, i, :, hh * HD:(hh + 1) * HD],
                                w[0].rearrange("(c h) i j -> h i c j", h=2)[hh]).then_inc(small_loaded, 16)
            g.dma_start(w2[:], cmp_w2[0].rearrange("v p d -> p v d")).then_inc(small_loaded, 16)
            g.dma_start(b2[:], cmp_b2[0].partition_broadcast(NCMP)).then_inc(small_loaded, 16)
            g.dma_start(rw[:, :, 0:4], router_group_w[0].rearrange("(p k) e -> p k e", p=P)).then_inc(small_loaded, 16)
            g.dma_start(rw[:, :, 4:KR], router_expert_w[0].rearrange("(p k) e -> p k e", p=P)).then_inc(small_loaded, 16)
            g.dma_start(rb[:, 0:4], router_group_b[0].partition_broadcast(P)).then_inc(small_loaded, 16)
            g.dma_start(rb[:, 4:KR], router_expert_b[0].partition_broadcast(P)).then_inc(small_loaded, 16)
            g.memset(zp[:, :, 0:2], 0.0).then_inc(pads, 1)
            g.memset(vbd[:], 0.0).then_inc(pads, 1)
            g.memset(pc[:], 0.0).then_inc(pads, 1)
        N_ROWDMA, N_SMALLDMA = 12, 10

        @block.scalar
        def _(act):
            a = nc.scalar
            act.dma_start(gain[:], mix_norm[0].partition_broadcast(P)).then_inc(gain_loaded, 16)
            done = [0]

            def splits(upto):
                for n in range(done[0], upto):
                    if n % 2 == 0:
                        loaded(act, SPLIT[n // 2])
                    high_free(act, n)
                    src, high = halves(n, wh)
                    a.copy(high, src).then_inc(hi_ready, 1)
                done[0] = max(done[0], upto)

            for t in range(TT):
                act.wait_ge(x_loaded[t], 16)
                a.activation(gate[:, 2 * t:2 * t + 2, :].rearrange("p k s -> p (k s)"), tok[:, t, :], ACT.Square,
                             accum_out=small[:, t:t + 1]).then_inc(x_squares, 1)
            act.wait_ge(x_mean, 1)
            a.activation(small[:, 4:6], small[:, 2:4], ACT.Sqrt).then_inc(x_root, 1)
            for i in range(4):
                full(act, f"xT{i}")
                a.copy(xh[:, 4 * (i // 2):4 * (i // 2) + 4, (i % 2) * P:(i % 2 + 1) * P],
                       bank3(f"xT{i}", 4, P)).then_inc(xh_ready, 1)
            splits(3)
            for t in range(TT):
                full(act, f"q{t}")
                freed(a.copy(q_sb[:, t, :], bank(f"q{t}")), f"q{t}")
            splits(5)
            for t in range(TT):
                name = f"kva{t}"
                full(act, name)
                for j in range(2):
                    a.copy(kdup[:, t, :, j, :], bank(name)[:, 0:256].rearrange("p (c d) -> p c d", d=HD))
                freed(a.copy(kvs[:, t, :], bank(name)[:, 256:512]), name)
            splits(7)
            for t in range(TT):
                name = f"kvb{t}"
                full(act, name)
                a.activation(ngs[:, t, :], bank(name)[:, 256:280], ACT.Tanh, scale=0.5)
                freed(a.copy(kvw[:, t, :], bank(name)[:, 0:256]), name)
            splits(8)
            for i, name in enumerate(("kc", "vc")):
                full(act, name)
                freed(a.copy(kcv[:, i], bank3(name, 2, S)), name)
            act.wait_ge(qk_mean, 1)
            a.activation(sq12[:], ssq[:], ACT.Sqrt).then_inc(qk_root, 1)
            act.wait_ge(lam_ready, 1)
            a.activation(small[:, 24:28], small[:, 20:24], ACT.Exp).then_inc(lam_exp, 1)
            splits(9)
            act.wait_ge(consts, 1)
            for i in range(2):
                full(act, f"rx{i}")
                freed(a.copy(rxp[:, 2 * i:2 * i + 2, 3:3 + S], bank3(f"rx{i}", 2, S)), f"rx{i}")
            splits(10)
            full(act, "hid")
            for kv in range(2):
                ins = a.activation(hid[:, kv, :], bank("hid")[:, kv * 32:kv * 32 + 30], ACT.Gelu_apprx_tanh,
                                   bias=pcol[:, ROWS["b1"] + kv:ROWS["b1"] + kv + 1])
            freed(ins, "hid")
            splits(11)
            act.wait_ge(x_normed, 2)
            for i in range(2):
                full(act, f"ry{i}")
                freed(a.activation(yT[:, 0, 2 * i:2 * i + 2, :], bank3(f"ry{i}", 2, S), ACT.Gelu_apprx_tanh), f"ry{i}")
            splits(12)
            act.wait_ge(kc_mean, 1)
            a.activation(small[0:NCMP, 70:72], small[0:NCMP, 68:70], ACT.Sqrt).then_inc(kc_root, 1)
            act.wait_ge(lru_scale, 1)
            for gname, dst, col in (("r", rg, 40), ("i", ig, 44)):
                for i in range(2):
                    name = f"{gname}{i}"
                    full(act, name)
                    for c in range(2):
                        ct = 2 * i + c
                        ins = a.activation(dst[:, ct, :], bank3(name, 2, S)[:, c, :], ACT.Tanh, scale=0.5,
                                           bias=small[:, col + ct:col + ct + 1])
                    freed(ins, name)
            act.wait_ge(bank_free[FI["r1"] % 4], FI["r1"] // 4 + 1)
            for ct in range(CT):
                a.activation(rr[:, ct, :], rg[:, ct, :], ACT.Exp, scale=small[:, 52 + ct:53 + ct],
                             bias=small[:, 52 + ct:53 + ct])
            splits(13)
            for ct in range(CT):
                ins = a.activation(rg[:, ct, :], rg[:, ct, :], ACT.Tanh, scale=small[:, 48 + ct:49 + ct],
                                   bias=small[:, 48 + ct:49 + ct])
            ins.then_inc(th_ready, 1)

            def exps(n):
                tt = UNITS[n][1]
                w = P * (tt + 1)
                for br in range(2):
                    act.wait_ge(scores_maxed, 2 * n + br + 1)
                    for hh in range(HG):
                        ins = a.activation(s_sb[:, br, hh, 0:w], s_sb[:, br, hh, 0:w], ACT.Exp,
                                           bias=nm[:, br, hh:hh + 1], accum_out=l_sb[:, br, hh:hh + 1])
                    ins.then_inc(scores_exped, 1)

            def turned(n):
                tt = UNITS[n][1]
                for sbk in range(tt + 1):
                    name = f"pt{n}_0{sbk}"
                    full(act, name)
                    freed(a.copy(pT[:, 0, sbk], bank3(name, HG, P)), name)
                full(act, f"ptc{n}")
                freed(a.copy(pTc[:], bank(f"ptc{n}")[:, 0:P]), f"ptc{n}")

            def output(n):
                g, tt = UNITS[n]
                full(act, f"o{n}")
                dst = yT[:, 1, 2 * g:2 * g + 2, tt * P:(tt + 1) * P]
                freed(a.copy(dst, bank3(f"o{n}", 2, P)), f"o{n}")

            def gates(b, half):
                if b != BR[0]:
                    last = f"p{BR[BR.index(b) - 1]}_{2 * half + 1}"
                    act.wait_ge(bank_free[FI[last] % 4], FI[last] // 4 + 1)
                for t in range(TT):
                    name = f"g{'ab'[half]}{b}_{t}"
                    full(act, name)
                    freed(a.activation(gate[:, 2 * half + t, :], bank(name), ACT.Tanh, scale=0.5), name)

            exps(0)
            for i in range(2):
                full(act, f"sb{i}")
                freed(a.copy(yT[:, 2, 2 * i:2 * i + 2, :], bank3(f"sb{i}", 2, S)), f"sb{i}")
            splits(14)
            act.wait_ge(negth_ready, 1)
            a.activation(root[:], rg[:], ACT.Sqrt, scale=0.25).then_inc(root_ready, 1)
            splits(15)
            for i in range(2):
                full(act, f"sc{i}")
                freed(a.copy(scc[:, 2 * i:2 * i + 2, :], bank3(f"sc{i}", 2, S)), f"sc{i}")
            splits(16)
            act.wait_ge(sc_shifted, 1)
            a.activation(pc[:, :, :, 0:NCMP], pc[:, :, :, 0:NCMP], ACT.Exp).then_inc(sc_exped, 1)
            splits(18)
            turned(0)
            output(0)
            exps(1)
            splits(20)
            gates(0, 0)
            turned(1)
            output(1)
            def y_high(i, ready):
                act.wait_ge(*ready)
                if i:
                    full(act, f"p{BR[i - 1]}_3")
                a.copy(yh[:], yT[:, BR[i]]).then_inc(yh_ready, 1)

            exps(2)
            splits(21)
            y_high(0, (y_rnn_ready, 1))
            splits(22)
            gates(0, 1)
            splits(24)
            turned(2)
            output(2)
            exps(3)
            splits(26)
            gates(2, 0)
            splits(27)
            y_high(1, (y_sc_ready, 1))
            splits(28)
            gates(2, 1)
            turned(3)
            output(3)
            act.dma_start(x1[:], x[0].rearrange("(t p) n -> p t n", p=P)).then_inc(x_again, 16)
            act.wait_ge(yl_ready, 1)
            act.dma_start(gain[:], ffn_norm[0].partition_broadcast(P)).then_inc(x_again, 16)
            splits(30)
            y_high(2, (bank_free[FI["o3"] % 4], FI["o3"] // 4 + 1))
            splits(32)
            gates(1, 0)
            splits(34)
            gates(1, 1)
            splits(36)
            for i in range(4):
                full(act, f"mT{i}")
                a.mul(xh[:, 4 * (i // 2):4 * (i // 2) + 4, (i % 2) * P:(i % 2 + 1) * P],
                      bank3(f"mT{i}", 4, P), 0.5).then_inc(xh_ready, 1)
            splits(len(ENDED))
            a.activation(small[:, 92:93], small[:, 4:5], ACT.Sqrt)
            for t in range(TT):
                for i in (t, t + 2):
                    act.wait_ge(bank_free[FI[f"wo{i}"] % 4], FI[f"wo{i}"] // 4 + 1)
                a.activation(tok[:, t, :], x1[:, t, :], ACT.Square, accum_out=small[:, 80 + t:81 + t]
                             ).then_inc(x2_squares, 1)
                act.wait_ge(x2_mean, t + 1)
                a.activation(small[:, 84 + t:85 + t], small[:, 82 + t:83 + t], ACT.Sqrt).then_inc(x2_root, 1)
            for t in range(TT):
                full(act, f"x2T{2 * t}")
                freed(a.copy(x2T[:, 0:4, t * P:(t + 1) * P], bank3(f"x2T{2 * t}", 4, P)), f"x2T{2 * t}")
            act.wait_ge(g_shifted, 1)
            a.activation(rt[:, 1, :, 0:4], rt[:, 0, :, 0:4], ACT.Exp).then_inc(g_exped, 1)
            act.wait_ge(m_shifted, 1)
            a.activation(rs[:, 8, :], rs[:, 7, :], ACT.Exp).then_inc(m_exped, 1)

            act.wait_ge(gather_done, 1)
            a.copy(xg[:, 0:4, :], xo[:, 0, :].rearrange("p (k s) -> p k s", k=4)).then_inc(xg_act, 1)
            act.wait_ge(rounds_ready, 1)
            nr = act.value_load(nrounds[0:1, 0:1], min_val=1, max_val=MAXR)
            with act.Fori(0, nr * NG) as it:
                act.wait_ge(kpair_done, it * 4 + 4)
                a.activation(hs[:], h_ps[:, 0:F], ACT.Silu).then_inc(silu_done, 1)
                act.wait_ge(gather_done, it * 2 + 3)
                a.copy(xg[:, 0:4, :], xo[:, 0, :].rearrange("p (k s) -> p k s", k=4)).then_inc(xg_act, 1)
                act.wait_ge(hT_done, it + 1)
                a.copy(hT[:], t_ps[:, 0:2 * P].rearrange("p (c s) -> p c s", c=2)).then_inc(hT_copied, 1)
                act.wait_ge(down_done, it * 2 + 1)
                a.copy(o_sb[:, 0:CB], xo[:, 0, :]).then_inc(o_act, 1)

        @block.vector
        def _(dve):
            v = nc.vector
            n = [0]
            last = [None]

            def do(ins):
                n[0] += 1
                ins.then_inc(dve_chain, 1)
                last[0] = (dve_chain, n[0])

            def signal(ins, s, value):
                ins.then_inc(s, 1)
                last[0] = (s, value)

            def free(ins, name):
                freed(ins, name)
                last[0] = (bank_free[FI[name] % 4], FI[name] // 4 + 1)

            def settle():
                dve.wait_ge(*last[0])

            def chain(ins):
                do(ins)
                settle()

            done = [0]

            def splits(upto):
                for m in range(done[0], upto):
                    dve.wait_ge(hi_ready, m + 1)
                    low_free(dve, m)
                    src, low = halves(m, wl)
                    signal(v.tensor_tensor(low, src, halves(m, wh)[1].bitcast(fp32), ALU.subtract), lo_ready, m + 1)
                done[0] = max(done[0], upto)

            def col(name, i=0, rows=slice(0, P)):
                return pcol[rows, ROWS[name] + i:ROWS[name] + i + 1]

            dve.wait_ge(x_squares, 2)
            signal(v.tensor_scalar(small[:, 2:4], small[:, 0:2], 1.0 / D, EPS, ALU.mult, ALU.add), x_mean, 1)
            settle()
            dve.wait_ge(x_root, 1)
            chain(v.reciprocal(small[:, 6:8], small[:, 4:6]))
            dve.wait_ge(gain_loaded, 16)
            for t in range(TT):
                signal(v.scalar_tensor_tensor(tok[:, t, :], tok[:, t, :], small[:, 6 + t:7 + t], gain[:],
                                              ALU.mult, ALU.mult), x_normed, t + 1)
            for i in range(4):
                dve.wait_ge(xh_ready, i + 1)
                c = slice(4 * (i // 2), 4 * (i // 2) + 4), slice((i % 2) * P, (i % 2 + 1) * P)
                free(v.tensor_tensor(xl[:, c[0], c[1]], bank3(f"xT{i}", 4, P), xh[:, c[0], c[1]].bitcast(fp32),
                                     ALU.subtract), f"xT{i}")
            splits(4)

            def wait_freed(eng, name):
                eng.wait_ge(bank_free[FI[name] % 4], FI[name] // 4 + 1)

            wait_freed(dve, "q1")
            heads = q_sb[:].rearrange("p t (h d) -> p (t h) d", d=HD)
            chain(v.tensor_tensor(sqs[:], q_sb[:], q_sb[:], ALU.mult))
            chain(v.tensor_reduce(ssq[:, :, 0:8], sqs[:].rearrange("p t (h d) -> p t h d", d=HD), AX.X, ALU.add))
            splits(6)
            for i, kk in enumerate((kvs, kvw)):
                wait_freed(dve, ("kva1", "kvb1")[i])
                if i:
                    splits(7)
                chain(v.tensor_tensor(sqs[:, :, 0:P], kk[:, :, 0:P], kk[:, :, 0:P], ALU.mult))
                chain(v.tensor_reduce(ssq[:, :, 8 + 2 * i:10 + 2 * i],
                                      sqs[:, :, 0:P].rearrange("p t (h d) -> p t h d", d=HD), AX.X, ALU.add))
            signal(v.tensor_scalar(ssq[:], ssq[:], 1.0 / HD, EPS, ALU.mult, ALU.add), qk_mean, 1)
            chain(v.tensor_scalar(ngs[:], ngs[:], 0.5, 0.5, ALU.mult, ALU.add))
            full(dve, "par")
            free(v.tensor_copy(pcol[:], bank("par")[:, 0:NROWS]), "par")
            settle()
            lam = pcol[:, ROWS["lam"]:ROWS["lam"] + CT]
            chain(v.tensor_scalar(small[:, 16:20], lam, -1.0, None, ALU.mult))
            signal(v.tensor_tensor(small[:, 20:24], small[:, 16:20], lam, ALU.min), lam_ready, 1)
            do(v.tensor_scalar(small[:, 40:44], pcol[:, ROWS["ba"]:ROWS["ba"] + CT], 0.5, None, ALU.mult))
            do(v.tensor_scalar(small[:, 44:48], pcol[:, ROWS["bx"]:ROWS["bx"] + CT], 0.5, None, ALU.mult))
            do(v.tensor_scalar(small[:, 60:61], col("qn"), HD ** -0.5, None, ALU.mult))
            splits(8)
            wait_freed(dve, "kc")
            wait_freed(dve, "vc")
            for kv in range(2):
                for j in range(2):
                    r = slice(j * HD, (j + 1) * HD)
                    for hi in range(2):
                        src = kcv[r, kv].rearrange("p g (m l j) -> p j l g m", m=CS, j=2)[:, j, :, :, hi:hi + NCMP]
                        lo = hi * 8
                        pe = pcol[r, ROWS["pe"] + kv * LP + lo:ROWS["pe"] + kv * LP + lo + 8]
                        ins = v.tensor_tensor(
                            cx[r, kv, lo:lo + 8, :].rearrange("p l (g n) -> p l g n", g=GROUPS), src,
                            bc(pe.unsqueeze(2).unsqueeze(3), [HD, 8, GROUPS, NCMP]), ALU.add)
                        if kv == 1 and j == 1 and hi == 1:
                            signal(ins, cx_ready, 1)
                        else:
                            do(ins)
            splits(9)
            dve.wait_ge(qk_root, 1)
            chain(v.reciprocal(sq12[:], sq12[:]))
            hv = q_sb[:].rearrange("p t (h d) -> p t h d", d=HD)
            do(v.tensor_tensor(hv, hv, bc(sq12[:, :, 0:HEADS].unsqueeze(3), [P, TT, HEADS, HD]), ALU.mult))
            for br, kk in enumerate((kvs, kvw)):
                for j in range(2):
                    c = HEADS + 2 * br
                    ins = v.tensor_tensor(kd[:, br, :, :, j * HD:(j + 1) * HD],
                                          kk[:, :, 0:P].rearrange("p t (g d) -> p t g d", d=HD),
                                          bc(sq12[:, :, c:c + 2].unsqueeze(3), [P, TT, GROUPS, HD]), ALU.mult)
                    if br == 1 and j == 1:
                        signal(ins, qk_normed, 1)
                    else:
                        do(ins)
            for t in range(TT):
                full(dve, f"qT{t}")
                free(v.tensor_scalar(qT[:, :, t * P:(t + 1) * P], bank3(f"qT{t}", CT, P), small[:, 60:61], None,
                                     ALU.mult), f"qT{t}")
            for i, name in enumerate(("kTs", "kTw")):
                full(dve, name)
                free(v.tensor_scalar(kT[:, i], bank3(name, GROUPS, S), col("kn", 1 + i), None, ALU.mult), name)
            splits(10)
            wait_freed(dve, "rx1")
            for k in range(RNN_TAPS):
                for ct in range(CT):
                    src = rxp[:, ct, k:k + S]
                    wk = col("cw", k * CT + ct)
                    if k == 0:
                        ins = v.tensor_scalar(u[:, ct, :], src, wk, col("cb", ct), ALU.mult, ALU.add)
                    else:
                        ins = v.scalar_tensor_tensor(u[:, ct, :], src, wk, u[:, ct, :], ALU.mult, ALU.add)
                    if k == RNN_TAPS - 1 and ct == CT - 1:
                        signal(ins, u_ready, 1)
                    else:
                        do(ins)
                settle()

            dve.wait_ge(lam_exp, 1)
            z, w, w2_, acc = (small[:, c:c + CT] for c in (24, 28, 32, 36))
            chain(v.tensor_scalar(w, z, 2.0, None, ALU.add))
            chain(v.reciprocal(w, w))
            chain(v.tensor_tensor(w, w, z, ALU.mult))
            chain(v.tensor_tensor(w2_, w, w, ALU.mult))
            chain(v.tensor_scalar(acc, w2_, 1.0 / 17, None, ALU.mult))
            for k in (15, 13, 11, 9, 7, 5, 3):
                chain(v.scalar_tensor_tensor(acc, acc, 1.0 / k, w2_, ALU.add, ALU.mult))
            chain(v.scalar_tensor_tensor(acc, acc, 1.0, w, ALU.add, ALU.mult))
            chain(v.tensor_scalar(small[:, 16:20], small[:, 16:20], 0.0, -2.0, ALU.max, ALU.mult))
            chain(v.scalar_tensor_tensor(small[:, 48:52], acc, -4.0, small[:, 16:20], ALU.mult, ALU.add))
            signal(v.tensor_scalar(small[:, 52:56], small[:, 48:52], 2.0, None, ALU.mult), lru_scale, 1)
            def maxima(n):
                tt = UNITS[n][1]
                w = P * (tt + 1)
                for br in range(2):
                    dve.wait_ge(scores_full, 2 * n + br + 1)
                    if n:
                        full(dve, f"ptc{n - 1}")
                    chain(v.tensor_tensor(s_sb[:, br].rearrange("p (h a) s -> p h a s", a=2)[:, :, :, 0:w],
                                          s_ps[br][:, :, :, 0:w],
                                          bc(cmask[:, 2 * P - w:2 * P].unsqueeze(1).unsqueeze(1), [P, 2, 2, w]), ALU.add))
                    signal(v.tensor_reduce(nm[:, br, :], s_sb[:, br, :, 0:w], AX.X, ALU.max, negate=True),
                           scores_maxed, 2 * n + br + 1)

            def probs(n):
                g, tt = UNITS[n]
                w = P * (tt + 1)
                for br in range(2):
                    dve.wait_ge(scores_exped, 2 * n + br + 1)
                    chain(v.reciprocal(l_sb[:, br, :], l_sb[:, br, :]))
                    gb = ngs[:, tt, :].rearrange("p (h b) -> p h b", b=3)[:, g * HG:(g + 1) * HG, br + 1]
                    chain(v.tensor_tensor(l_sb[:, br, :], l_sb[:, br, :], gb, ALU.mult))
                    signal(v.tensor_tensor(s_sb[:, br, :, 0:w], s_sb[:, br, :, 0:w],
                                           bc(l_sb[:, br, :].unsqueeze(2), [P, HG, w]), ALU.mult),
                           probs_ready, 2 * n + br + 1)

            def turned(n):
                tt = UNITS[n][1]
                for sbk in range(tt + 1):
                    name = f"pt{n}_1{sbk}"
                    full(dve, name)
                    free(v.tensor_copy(pT[:, 1, sbk], bank3(name, HG, P)), name)

            splits(12)
            dve.wait_ge(small_loaded, 16 * N_SMALLDMA)
            dve.wait_ge(pads, 3)
            full(dve, "cmp2")
            kv2 = bank("cmp2")[0:NCMP, 0:256].rearrange("p (v g d) -> p v g d", v=2, g=GROUPS)
            kc = kc_sb[0:NCMP]
            do(v.tensor_tensor(kc, kv2[:, 0], bc(b2[:, 0, :].unsqueeze(1), [NCMP, GROUPS, HD]), ALU.add))
            for hh in range(HG):
                ins = v.tensor_tensor(vbd[32 * hh:32 * hh + NCMP, :, hh, :], kv2[:, 1],
                                      bc(b2[:, 1, :].unsqueeze(1), [NCMP, GROUPS, HD]), ALU.add)
                if hh < HG - 1:
                    do(ins)
                else:
                    free(ins, "cmp2")
            settle()
            chain(v.tensor_tensor(kc_sq[0:NCMP], kc, kc, ALU.mult))
            chain(v.tensor_reduce(small[0:NCMP, 64:66], kc_sq[0:NCMP], AX.X, ALU.add))
            signal(v.tensor_scalar(small[0:NCMP, 68:70], small[0:NCMP, 64:66], 1.0 / HD, EPS, ALU.mult, ALU.add),
                   kc_mean, 1)
            maxima(0)
            dve.wait_ge(kc_root, 1)
            chain(v.reciprocal(small[0:NCMP, 72:74], small[0:NCMP, 70:72]))
            for j in range(2):
                ins = v.tensor_tensor(kcd[0:NCMP, :, j * HD:(j + 1) * HD], kc,
                                      bc(small[0:NCMP, 72:74].unsqueeze(2), [NCMP, GROUPS, HD]), ALU.mult)
                if j == 0:
                    do(ins)
                else:
                    signal(ins, kc_normed, 1)
            splits(14)
            full(dve, "kcT")
            free(v.tensor_scalar(cmpT[:, :, 0:NCMP], bank("kcT")[:, 0:32].rearrange("p (g n) -> p g n", g=2)[:, :, 0:NCMP],
                                 col("kn", 0), None, ALU.mult), "kcT")
            tmp = a_moe[:, 0:2 * CB]

            def merge(b, i):
                half, t = i // 2, i % 2
                name = f"p{b}_{i}"
                full(dve, name)
                wait_freed(dve, f"g{'ab'[half]}{b}_{t}")
                dst = tok[:, t, half * CB:(half + 1) * CB]
                if b == BR[0]:
                    free(v.scalar_tensor_tensor(dst, gate[:, i, :], 1.0, bank(name), ALU.add, ALU.mult), name)
                    return
                tm = tmp[:, (i % 2) * CB:(i % 2 + 1) * CB]
                free(v.scalar_tensor_tensor(tm, gate[:, i, :], 1.0, bank(name), ALU.add, ALU.mult), name)
                settle()
                ins = v.tensor_tensor(dst, dst, tm, ALU.add)
                if b == BR[2]:
                    signal(ins, merged_ready, i + 1)
                else:
                    do(ins)

            probs(0)
            dve.wait_ge(th_ready, 1)
            signal(v.tensor_scalar(rg[:], rg[:], -1.0, 1e-30, ALU.mult, ALU.max), negth_ready, 1)
            do(v.scalar_tensor_tensor(u[:], ig[:], 1.0, u[:], ALU.add, ALU.mult))
            splits(15)
            pcv = pc[:, :, :, 0:NCMP]
            for a in range(2):
                name = f"Sc{a}"
                full(dve, name)
                scp = bank(name)[:, 0:TT * HEADS * 8].rearrange("p (t h n) -> p t h n", t=TT, h=HEADS // 2)
                for t in range(TT):
                    ins = v.tensor_tensor(pc[:, t].rearrange("p (h a) n -> p h a n", a=2)[:, :, a, 0:NCMP],
                                          scp[:, t, :, 0:NCMP],
                                          bc(nmask[:, t, :].unsqueeze(1), [P, HEADS // 2, NCMP]), ALU.add)
                    if t == 0:
                        do(ins)
                    else:
                        free(ins, name)
            settle()
            c0, c1 = coef[:, 0, :].rearrange("p (t h) -> p t h", t=TT), coef[:, 1, :].rearrange("p (t h) -> p t h", t=TT)
            chain(v.tensor_reduce(c0, pcv, AX.X, ALU.max))
            signal(v.tensor_tensor(pcv, pcv, bc(c0.unsqueeze(3), [P, TT, HEADS, NCMP]), ALU.subtract), sc_shifted, 1)
            splits(16)
            dve.wait_ge(sc_exped, 1)
            chain(v.tensor_reduce(c0, pcv, AX.X, ALU.add))
            chain(v.reciprocal(c0, c0))
            chain(v.tensor_tensor(c1, ngs[:].rearrange("p t (h b) -> p t h b", b=3)[:, :, :, 0],
                                  bc(ngany[:].unsqueeze(2), [P, TT, HEADS]), ALU.mult))
            chain(v.tensor_tensor(c0, c0, c1, ALU.mult))
            signal(v.tensor_tensor(pcv, pcv, bc(c0.unsqueeze(3), [P, TT, HEADS, NCMP]), ALU.mult), pc_ready, 1)
            splits(17)
            wait_freed(dve, "sc1")
            for i in range(2):
                full(dve, f"sh{i}")
                free(v.tensor_tensor(zp[:, 2 * i:2 * i + 2, 2:2 + S], bank3(f"sh{i}", 2, S),
                                     scc[:, 2 * i:2 * i + 2, :], ALU.mult), f"sh{i}")
            turned(0)
            splits(18)
            maxima(1)
            chain(v.scalar_tensor_tensor(u[:], rr[:], 1.0, u[:], ALU.add, ALU.mult))
            probs(1)
            splits(19)
            dve.wait_ge(root_ready, 1)
            chain(v.tensor_tensor(u[:], u[:], root[:], ALU.mult))
            turned(1)
            splits(20)
            maxima(2)
            for ct in range(CT):
                do(v.tensor_tensor_scan(rg[:, ct, :], rr[:, ct, :], u[:, ct, :], 0.0, ALU.mult, ALU.add))
            settle()
            wait_freed(dve, "ry1")
            signal(v.tensor_tensor(yT[:, 0], yT[:, 0], rg[:], ALU.mult), y_rnn_ready, 1)
            def y_low(i):
                dve.wait_ge(yh_ready, i + 1)
                signal(v.tensor_tensor(yl[:], yT[:, BR[i]], yh[:].bitcast(fp32), ALU.subtract), yl_ready, i + 1)

            probs(2)
            y_low(0)
            splits(21)
            for k in range(SC_TAPS):
                for ct in range(CT):
                    src = zp[:, ct, k:k + S]
                    wk = col("sw", k * CT + ct)
                    if k == 0:
                        do(v.tensor_scalar(scc[:, ct, :], src, wk, None, ALU.mult))
                    else:
                        do(v.scalar_tensor_tensor(scc[:, ct, :], src, wk, scc[:, ct, :], ALU.mult, ALU.add))
                settle()
            splits(22)
            for i in range(4):
                merge(0, i)
            turned(2)
            splits(23)
            maxima(3)
            splits(24)
            probs(3)
            wait_freed(dve, "sb1")
            signal(v.tensor_tensor(yT[:, 2], yT[:, 2], scc[:], ALU.mult), y_sc_ready, 1)
            splits(26)
            y_low(1)
            splits(27)
            turned(3)
            splits(28)
            merge(2, 0)
            merge(2, 1)
            splits(29)
            merge(2, 2)
            merge(2, 3)
            splits(30)
            y_low(2)
            splits(34)
            merge(1, 0)
            merge(1, 1)
            splits(35)
            merge(1, 2)
            merge(1, 3)
            splits(36)
            for i in range(4):
                dve.wait_ge(xh_ready, 4 + i + 1)
                c = slice(4 * (i // 2), 4 * (i // 2) + 4), slice((i % 2) * P, (i % 2 + 1) * P)
                free(v.scalar_tensor_tensor(xl[:, c[0], c[1]], bank3(f"mT{i}", 4, P), 0.5,
                                            xh[:, c[0], c[1]].bitcast(fp32), ALU.mult, ALU.subtract), f"mT{i}")
            splits(len(ENDED))
            dve.wait_ge(x_again, 32)
            for i in range(4):
                half, t = i // 2, i % 2
                full(dve, f"wo{i}")
                dst = x1[:, t, half * CB:(half + 1) * CB]
                free(v.tensor_tensor(dst, dst, bank(f"wo{i}"), ALU.add), f"wo{i}")
                if half == 0:
                    continue
                dve.wait_ge(x2_squares, t + 1)
                signal(v.tensor_scalar(small[:, 82 + t:83 + t], small[:, 80 + t:81 + t], 1.0 / D, EPS, ALU.mult, ALU.add),
                       x2_mean, t + 1)
                dve.wait_ge(x2_root, t + 1)
                chain(v.reciprocal(small[:, 86 + t:87 + t], small[:, 84 + t:85 + t]))
                signal(v.scalar_tensor_tensor(tok[:, t, :].rearrange("p (k q) -> p q k", k=KD),
                                              x1[:, t, :].rearrange("p (q k) -> p q k", k=KD),
                                              small[:, 86 + t:87 + t], gain[:].rearrange("p (q k) -> p q k", k=KD),
                                              ALU.mult, ALU.mult), x2_normed, t + 1)
            for t in range(TT):
                name = f"x2T{2 * t + 1}"
                full(dve, name)
                free(v.tensor_copy(x2T[:, 4:8, t * P:(t + 1) * P], bank3(name, 4, P)), name)
            for t in range(TT):
                full(dve, f"rl{t}")
                free(v.tensor_tensor(lg[:, t, :], bank(f"rl{t}")[:, 0:KR], rb[:], ALU.add), f"rl{t}")
            settle()

            def rtv(i, m=E):
                return rt[:, i, :, 0:m]

            def wide(ap, m):
                return bc(ap.unsqueeze(2), [P, TT, m])

            def first(values, top, m, key, dst):
                chain(v.tensor_tensor(rtv(key, m), values, wide(rs[:, top, :], m), ALU.is_equal))
                chain(v.tensor_tensor(rtv(key, m), rtv(key, m), bc(desc[:, 0:m].unsqueeze(1), [P, TT, m]), ALU.mult))
                chain(v.tensor_reduce(rs[:, 11, :], rtv(key, m), AX.X, ALU.max))
                chain(v.tensor_tensor(rtv(dst, m), rtv(key, m), wide(rs[:, 11, :], m), ALU.is_equal))

            gl, el = lg[:, :, 0:4], lg[:, :, 4:KR]
            chain(v.tensor_reduce(rs[:, 0, :], gl, AX.X, ALU.max))
            signal(v.tensor_tensor(rtv(0, 4), gl, wide(rs[:, 0, :], 4), ALU.subtract), g_shifted, 1)
            first(gl, 0, 4, 2, 3)
            dve.wait_ge(g_exped, 1)
            chain(v.tensor_reduce(rs[:, 1, :], rtv(1, 4), AX.X, ALU.add))
            do(v.reciprocal(rs[:, 2, :], rs[:, 1, :]))
            do(v.tensor_scalar(rtv(4, 4), rtv(3, 4), 1.0, -NEG, ALU.subtract, ALU.mult))
            settle()

            def by_group(ap):
                return ap.rearrange("p t (g e) -> p t g e", g=4)

            chain(v.tensor_tensor(by_group(rtv(5)), by_group(el), bc(rtv(3, 4).unsqueeze(3), [P, TT, 4, 8]), ALU.mult))
            chain(v.tensor_tensor(by_group(rtv(5)), by_group(rtv(5)), bc(rtv(4, 4).unsqueeze(3), [P, TT, 4, 8]), ALU.add))
            chain(v.tensor_reduce(rs[:, 5, :], rtv(5), AX.X, ALU.max))
            first(rtv(5), 5, E, 6, 7)
            chain(v.scalar_tensor_tensor(rtv(5), rtv(7), 2 * NEG, rtv(5), ALU.mult, ALU.add))
            chain(v.tensor_reduce(rs[:, 6, :], rtv(5), AX.X, ALU.max))
            signal(v.tensor_tensor(rs[:, 7, :], rs[:, 6, :], rs[:, 5, :], ALU.subtract), m_shifted, 1)
            first(rtv(5), 6, E, 6, 8)
            signal(v.tensor_tensor(rtv(9), rtv(7), rtv(8), ALU.add), picks_ready, 1)
            dve.wait_ge(m_exped, 1)
            chain(v.tensor_scalar(rs[:, 9, :], rs[:, 8, :], 1.0, None, ALU.add))
            chain(v.reciprocal(rs[:, 9, :], rs[:, 9, :]))
            chain(v.tensor_tensor(rs[:, 9, :], rs[:, 9, :], rs[:, 2, :], ALU.mult))
            chain(v.tensor_tensor(rs[:, 10, :], rs[:, 9, :], rs[:, 8, :], ALU.mult))
            do(v.tensor_tensor(rtv(7), rtv(7), wide(rs[:, 9, :], E), ALU.mult))
            do(v.tensor_tensor(rtv(8), rtv(8), wide(rs[:, 10, :], E), ALU.mult))
            settle()
            chain(v.tensor_tensor(rtv(10), rtv(7), rtv(8), ALU.add))
            full(dve, "pos")
            pp = bank("pos")[:, 0:TT * E].rearrange("p (t e) -> p t e", t=TT)
            do(v.tensor_reduce(small[:, 100:101], bank("pos")[:, TT * E:3 * E], AX.X, ALU.max))
            free(v.scalar_tensor_tensor(rtv(11), pp, 1.0, rtv(9), ALU.add, ALU.mult), "pos")
            settle()
            chain(v.tensor_scalar(rtv(11), rtv(11), -1.0, None, ALU.add))
            for t in range(TT):
                do(v.tensor_tensor(posx[:, t, 0:MAXR * E].rearrange("p (r e) -> p r e", r=MAXR),
                                   bc(rt[:, 11, t, :].unsqueeze(1), [P, MAXR, E]),
                                   bc(thr[:].unsqueeze(2), [P, MAXR, E]), ALU.subtract))
                do(v.tensor_copy(combx[:, t, 0:MAXR * E].rearrange("p (r e) -> p r e", r=MAXR),
                                 bc(rt[:, 10, t, :].unsqueeze(1), [P, MAXR, E])))
            do(v.memset(posx[:, :, MAXR * E:], -1.0))
            do(v.memset(combx[:, :, MAXR * E:], 0.0))
            do(v.tensor_scalar(small[0:1, 104:112], thr[0:1, :], small[0:1, 100:101], None, ALU.is_lt))
            settle()

            def one_hot(c, value):
                signal(v.tensor_tensor(hot[:], bc(iot[:].unsqueeze(1).unsqueeze(1), [P, TT, EG, SLOTS]),
                                       bc(posx[:, :, c].unsqueeze(3), [P, TT, EG, SLOTS]), ALU.is_equal),
                       hot_ready, value)

            def one_hot_weighted(c, value):
                settle()
                signal(v.tensor_tensor(hotw[:], hot[:], bc(combx[:, :, c].unsqueeze(3), [P, TT, EG, SLOTS]), ALU.mult),
                       hotw_ready, value)

            one_hot(slice(0, EG), 1)
            one_hot_weighted(slice(0, EG), 1)
            chain(v.tensor_reduce(small[0:1, 112:113], small[0:1, 104:112], AX.X, ALU.add))
            signal(v.tensor_copy(nrounds[:], small[0:1, 112:113]), rounds_ready, 1)
            dve.wait_ge(gather_done, 2)
            v.tensor_copy(xg[:, 4:8, :], xo[:, 1, :].rearrange("p (k s) -> p k s", k=4)).then_inc(xg_dve, 1)
            dve.wait_ge(rounds_ready, 1)
            nr = dve.value_load(nrounds[0:1, 0:1], min_val=1, max_val=MAXR)
            with dve.Fori(0, nr * NG) as it:
                dve.wait_ge(hotw_ready, it + 1)
                one_hot(bass.ds(it * EG + EG, EG), it + 2)
                dve.wait_ge(hotT_done, it + 1)
                v.tensor_copy(hotT[:], t_ps[:, 2 * P:4 * P].rearrange("p (t q) -> p t q", t=TT)).then_inc(hotT_copied, 1)
                dve.wait_ge(silu_done, it + 1)
                v.tensor_tensor(h[:], hs[:], h_ps[:, F:2 * F], ALU.mult).then_inc(h_ready, 1)
                dve.wait_ge(gather_done, it * 2 + 4)
                v.tensor_copy(xg[:, 4:8, :], xo[:, 1, :].rearrange("p (k s) -> p k s", k=4)).then_inc(xg_dve, 1)
                one_hot_weighted(bass.ds(it * EG + EG, EG), it + 2)
                dve.wait_ge(down_done, it * 2 + 2)
                v.tensor_copy(o_sb[:, CB:], xo[:, 1, :]).then_inc(o_dve, 1)
            for i in range(4):
                t, hf = i // 2, i % 2
                if i == 0:
                    dve.wait_ge(scatter_done, nr * (2 * NG))
                c = slice(hf * CB, (hf + 1) * CB)
                v.tensor_tensor(x1[:, t, c], y_ps[:, i, :], x1[:, t, c], ALU.add).then_inc(y_ready, 1)

        @block.tensor
        def _(pe):
            t_ = nc.tensor

            def open_(name):
                n = FI[name]
                if n >= 4:
                    pe.wait_ge(bank_free[n % 4], n // 4)

            def close(ins, name):
                ins.then_inc(bank_full, 1)

            def wait_freed(name):
                pe.wait_ge(bank_free[FI[name] % 4], FI[name] // 4 + 1)


            def split_block(load, channels=False, turned=None):
                names = MADE[load]
                n = {"kvb": KVB}.get(load, CB)
                for hf in range(2):
                    m = SI[load] + hf
                    if turned:
                        wait_freed(f"{turned}{2 * hf}")
                        wait_freed(f"{turned}{2 * hf + 1}")
                    for low in range(2):
                        pe.wait_ge((hi_ready, lo_ready)[low], m + 1)
                        wv = halves(m, (wh, wl)[low])[1]
                        for i, name in enumerate(names):
                            if hf == 0 and not low:
                                open_(name)
                            for c in range(2 if channels else 1):
                                for k in range(KH):
                                    kk = hf * KH + k
                                    for xp in ((xh,) if low else (xh, xl)):
                                        start = kk == 0 and c == 0 and xp is xh and not low
                                        stop = kk == KD - 1 and low == 1
                                        if channels:
                                            ct = 2 * i + c
                                            ins = t_.matmul(bank(name)[:, c * S:(c + 1) * S],
                                                            wv[:, k, ct * P:(ct + 1) * P], xp[:, kk, :],
                                                            start=start, stop=stop, skip_group_check=True)
                                        else:
                                            ins = t_.matmul(bank(name)[:, 0:n], xp[:, kk, i * P:(i + 1) * P],
                                                            wv[:, k, :], start=start, stop=stop)
                            if hf == 1 and low:
                                close(ins, name)
                        if not low:
                            ins.then_inc(hi_used, 1)
                        elif hf == 0:
                            ins.then_inc(lo_used, 1)

            pe.wait_ge(ident_ready, 1)

            def turn_tokens(names, ready=None, by_half=True):
                for i, name in names:
                    t, k0 = (i % 2, 4 * (i // 2)) if by_half else (i // 2, 4 * (i % 2))
                    if ready is not None:
                        ready(i)
                    open_(name)
                    for k in range(4):
                        ins = t_.transpose(bank(name)[:, k * P:(k + 1) * P], tok[:, t, (k0 + k) * P:(k0 + k + 1) * P],
                                           ident[:, :])
                    close(ins, name)

            turn_tokens([(i, f"xT{i}") for i in range(4)], lambda i: pe.wait_ge(x_normed, i % 2 + 1))
            split_block("q", turned="xT")
            split_block("kva")
            split_block("kvb")
            wait_freed("kva1")
            for i, name in enumerate(("kc", "vc")):
                open_(name)
                for g in range(GROUPS):
                    for t in range(TT):
                        ins = t_.transpose(bank(name)[:, g * S + t * P:g * S + (t + 1) * P],
                                           kdup[:, t, i * GROUPS + g].rearrange("p j d -> p (j d)"), ident[:, :])
                close(ins, name)
            pe.wait_ge(consts, 1)
            pe.wait_ge(rows_loaded, 16 * N_ROWDMA)
            open_("par")
            close(t_.transpose(bank("par")[:, 0:P], prow[:, :], ident[:, :]), "par")
            split_block("rx", channels=True)
            loaded(pe, "cmp")
            pe.wait_ge(cx_ready, 1)
            open_("hid")
            w1 = slot("cmp")[:, :].rearrange("p (v l n) -> p v l n", v=2, l=LP)
            for kv in range(2):
                for lp in range(LP):
                    ins = t_.matmul(bank("hid")[:, kv * 32:kv * 32 + 30], w1[:, kv, lp, :], cx[:, kv, lp, :],
                                    start=lp == 0, stop=lp == LP - 1)
            close(ins, "hid")

            pe.wait_ge(qk_normed, 1)
            for t in range(TT):
                open_(f"qT{t}")
                for c in range(CT):
                    ins = t_.transpose(bank(f"qT{t}")[:, c * P:(c + 1) * P], q_sb[:, t, c * P:(c + 1) * P], ident[:, :])
                close(ins, f"qT{t}")
            for br, name in enumerate(("kTs", "kTw")):
                open_(name)
                for g in range(GROUPS):
                    for t in range(TT):
                        ins = t_.transpose(bank(name)[:, g * S + t * P:g * S + (t + 1) * P], kd[:, br, t, g, :],
                                           ident[:, :])
                close(ins, name)
            def scores(n):
                g, tt = UNITS[n]
                w = P * (tt + 1)
                for br in range(2):
                    if n:
                        pe.wait_ge(scores_maxed, 2 * n + br - 1)
                    for hh in range(HG):
                        hd = g * HG + hh
                        r = slice((hd % 2) * HD, (hd % 2 + 1) * HD)
                        ins = t_.matmul(s_ps[br][:, hh // 2, hh % 2, 0:w], qT[r, hd // 2, tt * P:(tt + 1) * P], kT[r, br, g, 0:w],
                                        start=True, stop=True)
                    ins.then_inc(scores_full, 1)

            split_block("ry", channels=True)
            wait_freed("kTw")
            wait_freed("hid")
            scores(0)
            pe.wait_ge(small_loaded, 16 * N_SMALLDMA)
            open_("cmp2")
            for kv in range(2):
                for g in range(GROUPS):
                    c0 = (kv * GROUPS + g) * HD
                    ins = t_.matmul(bank("cmp2")[0:NCMP, c0:c0 + HD], hid[:, kv, g * NCMP:(g + 1) * NCMP], w2[:, kv, :],
                                    start=True, stop=True)
            close(ins, "cmp2")
            pe.wait_ge(u_ready, 1)
            for i, gname in enumerate("ri"):
                for hf in range(2):
                    name = f"{gname}{hf}"
                    open_(name)
                    for c in range(2):
                        ct = 2 * hf + c
                        ins = t_.matmul(bank(name)[:, c * S:(c + 1) * S], wbd[:, i, ct, :], u[:, ct, :],
                                        start=True, stop=True)
                    close(ins, name)
            split_block("sb", channels=True)
            pe.wait_ge(kc_normed, 1)
            open_("kcT")
            for g in range(GROUPS):
                ins = t_.transpose(bank("kcT")[:, g * 16:g * 16 + NCMP], kcd[0:NCMP, g, :], ident[0:NCMP, 0:NCMP])
            close(ins, "kcT")
            split_block("sc", channels=True)
            wait_freed("kcT")
            for a in range(2):
                open_(f"Sc{a}")
                for tt in range(TT):
                    for hp in range(HEADS // 2):
                        r = slice(a * HD, (a + 1) * HD)
                        c0 = (tt * HEADS // 2 + hp) * 16
                        ins = t_.matmul(bank(f"Sc{a}")[:, c0:c0 + NCMP], qT[r, hp, tt * P:(tt + 1) * P],
                                        cmpT[r, 2 * hp // HG, 0:NCMP], start=True, stop=True)
                close(ins, f"Sc{a}")

            def attend(n):
                g, tt = UNITS[n]
                for br in range(2):
                    pe.wait_ge(probs_ready, 2 * n + br + 1)
                    for sbk in range(tt + 1):
                        name = f"pt{n}_{br}{sbk}"
                        open_(name)
                        for hh in range(HG):
                            ins = t_.transpose(bank(name)[:, hh * P:(hh + 1) * P],
                                               s_sb[:, br, hh, sbk * P:(sbk + 1) * P], ident[:, :])
                        close(ins, name)
                if n == 0:
                    pe.wait_ge(pc_ready, 1)
                name = f"ptc{n}"
                open_(name)
                close(t_.transpose(bank(name)[:, 0:P], pc[:, tt, g * HG:(g + 1) * HG, :].rearrange("p h n -> p (h n)"),
                                   ident[:, :]), name)
                name = f"o{n}"
                open_(name)
                for src in fills_of_unit(n)[:-1]:
                    wait_freed(src)
                for hh in range(HG):
                    dst = bank(name)[(hh % 2) * HD:(hh % 2 + 1) * HD, (hh // 2) * P:(hh // 2 + 1) * P]
                    first = True
                    for br, vv in ((0, kvs), (1, kvw)):
                        for sbk in range(tt + 1):
                            t_.matmul(dst, vv[:, sbk, P + g * HD:P + (g + 1) * HD], pT[:, br, sbk, hh, :],
                                      start=first, stop=False)
                            first = False
                    ins = t_.matmul(dst, vbd[:, g, hh, :], pTc[:], start=False, stop=True)
                close(ins, name)

            split_block("sh", channels=True)
            attend(0)
            scores(1)

            def gates(b, half):
                split_block(f"g{'ab'[half]}{b}")

            def product(i):
                b = BR[i]
                pe.wait_ge(yl_ready, i + 1)
                for hf in range(2):
                    m = SI[f"w{b}"] + hf
                    for low in range(2):
                        pe.wait_ge((hi_ready, lo_ready)[low], m + 1)
                        w = halves(m, (wh, wl)[low])[1]
                        for t in range(TT):
                            name = f"p{b}_{2 * hf + t}"
                            if not low:
                                open_(name)
                            for k in range(CT):
                                for yp in ((yh,) if low else (yh, yl)):
                                    ins = t_.matmul(bank(name), yp[:, k, t * P:(t + 1) * P], w[:, k, :],
                                                    start=k == 0 and yp is yh and not low, stop=k == CT - 1 and low == 1)
                            if low:
                                close(ins, name)
                        if not low:
                            ins.then_inc(hi_used, 1)

            gates(0, 0)
            attend(1)
            scores(2)
            gates(0, 1)
            product(0)
            attend(2)
            scores(3)
            gates(2, 0)
            gates(2, 1)
            attend(3)
            product(1)
            gates(1, 0)
            gates(1, 1)
            product(2)
            pe.wait_ge(merged_ready, 4)
            turn_tokens([(i, f"mT{i}") for i in range(4)])
            split_block("wo0", turned="mT")
            split_block("wo1")
            for t in range(TT):
                pe.wait_ge(x2_normed, t + 1)
                turn_tokens([(i, f"x2T{i}") for i in (2 * t, 2 * t + 1)], by_half=False)
            for t in range(TT):
                wait_freed(f"x2T{2 * t}")
                wait_freed(f"x2T{2 * t + 1}")
                open_(f"rl{t}")
                for k in range(KD):
                    ins = t_.matmul(bank(f"rl{t}")[:, 0:KR], x2T[:, k, t * P:(t + 1) * P], rw[:, k, :],
                                    start=k == 0, stop=k == KD - 1)
                close(ins, f"rl{t}")

            def zero(name):
                wait_freed(name)
                t_.matmul(y_ps[:, FI[name] % 4, :], nmask[0:1, 1, 0:1].to_broadcast([1, P]),
                          cmask[0:1, 0:1].to_broadcast([1, CB]), start=True, stop=True)

            for name in ("x2T2", "x2T3", "rl0", "rl1"):
                if FI[name] % 4 != FI["pos"] % 4:
                    zero(name)
            pe.wait_ge(picks_ready, 1)
            open_("pos")
            A = rt[:, 9]
            t_.matmul(bank("pos")[:, 0:E], tri[:, :], A[:, 0, :], start=True, stop=True)
            t_.matmul(bank("pos")[:, E:2 * E], tri[:, :], A[:, 1, :], start=True, stop=False)
            t_.matmul(bank("pos")[:, E:2 * E], ones[:, :], A[:, 0, :], start=False, stop=True)
            t_.matmul(bank("pos")[:, 2 * E:3 * E], ones[:, :], A[:, 0, :], start=True, stop=False)
            close(t_.matmul(bank("pos")[:, 2 * E:3 * E], ones[:, :], A[:, 1, :], start=False, stop=True), "pos")

            def gather(value):
                pe.wait_ge(hot_ready, value)
                hv = hot[:].rearrange("p t e s -> p t (e s)")
                for b in range(2):
                    for k in range(4):
                        for t in range(TT):
                            ins = t_.matmul(xo[:, b, k * P:(k + 1) * P], tok[:, t, (4 * b + k) * P:(4 * b + k + 1) * P],
                                            hv[:, t, :], start=t == 0, stop=t == TT - 1)
                    ins.then_inc(gather_done, 1)

            gather(1)
            zero("pos")
            pe.wait_ge(rounds_ready, 1)
            nr = pe.value_load(nrounds[0:1, 0:1], min_val=1, max_val=MAXR)
            with pe.Fori(0, nr * (NG // 2)) as i:
                for odd_group in (False, True):
                    it = i * 2 + int(odd_group)
                    pe.wait_ge(xg_act, it + 1)
                    pe.wait_ge(xg_dve, it + 1)
                    for j in range(4):
                        w, is_full = place(j, odd_group)
                        pe.wait_ge(is_full, (i if j < NDOUBLE else it) * 32 + 32)
                        w = w.rearrange("p (m e k f) -> p e k m f", m=2, e=EG, k=2)
                        for k in range(2):
                            for e in range(EG):
                                ins = t_.matmul(h_ps[e * SLOTS:(e + 1) * SLOTS, :].rearrange("p (m f) -> p m f", m=2),
                                                xg[:, 2 * j + k, e * SLOTS:(e + 1) * SLOTS], w[:, e, k],
                                                start=(j == 0 and k == 0), stop=(j == 3 and k == 1),
                                                skip_group_check=True)
                        ins.then_inc(kpair_done, 1)
                    pe.wait_ge(hotw_ready, it + 1)
                    for t in range(TT):
                        ins = t_.transpose(t_ps[:, (2 + t) * P:(3 + t) * P], hotw[:, t].rearrange("p e s -> p (e s)"),
                                           ident[:, :])
                    ins.then_inc(hotT_done, 1)
                    gather(it + 2)
                    pe.wait_ge(h_ready, it + 1)
                    for c in range(2):
                        ins = t_.transpose(t_ps[:, c * P:(c + 1) * P], h[:].rearrange("p (q c) -> p c q", c=2)[:, c, :],
                                           ident[:, :])
                    ins.then_inc(hT_done, 1)
                    pe.wait_ge(hT_copied, it + 1)
                    for hf in range(2):
                        pe.wait_ge(even_full[4 + hf], it * 32 + 32)
                        pe.wait_ge((xg_act, xg_dve)[hf], it + 2)
                        w = even[4 + hf].rearrange("p (e c n) -> p e c n", e=EG, c=2)
                        for c in range(2):
                            for e in range(EG):
                                ins = t_.matmul(xo[e * SLOTS:(e + 1) * SLOTS, hf, :], hT[:, c, e * SLOTS:(e + 1) * SLOTS],
                                                w[:, e, c, :], start=c == 0, stop=c == 1, skip_group_check=True)
                        ins.then_inc(down_done, 1)
                    pe.wait_ge(hotT_copied, it + 1)
                    for hf in range(2):
                        pe.wait_ge((o_act, o_dve)[hf], it + 1)
                        for t in range(TT):
                            ins = t_.matmul(y_ps[:, 2 * t + hf, :], hotT[:, t, :], o_sb[:, hf * CB:(hf + 1) * CB],
                                            start=False, stop=False, skip_group_check=True)
                        ins.then_inc(scatter_done, 1)


NAMES = ['x', 'mix_norm', 'w_in', 'rnn_conv_w', 'rnn_conv_b', 'rg_wa', 'rg_ba', 'rg_wx', 'rg_bx', 'rg_lambda',
         'cmp_pe', 'cmp_w1', 'cmp_b1', 'cmp_w2', 'cmp_b2', 'q_norm', 'k_norm', 'sc_conv_w',
         'w_rnn_out', 'w_nsa_out', 'w_sc_out', 'w_out', 'ffn_norm',
         'router_group_w', 'router_group_b', 'router_expert_w', 'router_expert_b',
         'exp_w_gate', 'exp_w_up', 'exp_w_down']


def kernel(**inputs):
    import concourse.bacc as bacc
    from concourse.bass_utils import run_bass_kernel_spmd

    nc = bacc.Bacc("TRN2", target_bir_lowering=False, num_devices=1)
    arrays, args = {}, []
    for name in NAMES:
        a = np.ascontiguousarray(inputs[name])
        arrays[f"in_{name}"] = a
        args.append(nc.dram_tensor(f"in_{name}", a.shape, mybir.dt.from_np(a.dtype), kind="ExternalInput").ap())
    args.append(nc.dram_tensor("out_0", (1, S, D), fp32, kind="ExternalOutput").ap())
    trunk(nc, *args)
    r = run_bass_kernel_spmd(nc, [arrays], core_ids=[0])
    return r.results[0]["out_0"]
```
